# Optimizing a Trainium2 kernel written in Bass

```python
import math
import jax
import jax.numpy as jnp
from jax import lax
import numpy as np

D_MODEL = 1024
BATCH = 1
SEQ = 256
DEPTH = 2

GRID_W = 64
CTX_LEN = 256
N_BRANCH = 4
BR_W = 512
A_HEADS = 4
A_DQK = 64
A_DV = 2 * A_DQK
A_QBLOCK = 128
ROPE_BASE = 10000.0
HY_W = BR_W
HY_ORDER = 2
HY_SHORT = 3
HY_BANDS = 16
HY_EMB = 1 + 2 * HY_BANDS
HY_HID = 64
HY_MIN_DECAY = math.log(1e-2) / 1.5
HY_MAX_DECAY = math.log(1e-2) / 0.3
FN_W = BR_W
FN_GROUPS = 4
DN_HEADS = 4
DN_DK = 128
DN_DV = 128
DN_SHORT = 3
DN_CHUNK = 64
D_FF = 4 * D_MODEL
EPS = 1e-6

OFF_AQ = 0
OFF_AK = OFF_AQ + A_HEADS * 2 * A_DQK
OFF_AV = OFF_AK + A_HEADS * 2 * A_DQK
OFF_HY = OFF_AV + A_HEADS * A_DV
OFF_FN = OFF_HY + (HY_ORDER + 1) * HY_W
OFF_DN = OFF_FN + FN_W
OFF_DZ = OFF_DN + DN_HEADS * (2 * DN_DK + DN_DV)
OFF_DA = OFF_DZ + DN_HEADS * DN_DV
OFF_DB = OFF_DA + 2 * DN_HEADS
N_IN = OFF_DB + 2 * DN_HEADS

kernel_name = 'hybrid_diffattn_hyena_fnet_gdn_dit'

F32 = jnp.float32

def rmsnorm(x, w):
    xf = x.astype(F32)
    y = xf * lax.rsqrt(jnp.mean(xf * xf, axis=-1, keepdims=True) + EPS)
    return (y * w.astype(F32)).astype(x.dtype)

def l2norm(x):
    return x * lax.rsqrt(jnp.sum(x * x, axis=-1, keepdims=True) + EPS)

def centred_conv(u, w):
    k = w.shape[0]
    r = k // 2
    length = u.shape[1]
    up = jnp.pad(u, ((0, 0), (r, r), (0, 0)))
    out = up[:, 0:length] * w[0]
    for i in range(1, k):
        out = out + up[:, i:i + length] * w[i]
    return out

def axial_rope_tables(length):
    rows = length // GRID_W
    row = jnp.repeat(jnp.arange(rows, dtype=F32), GRID_W)
    col = jnp.tile(jnp.arange(GRID_W, dtype=F32), rows)
    n_freq = A_DQK // 4
    inv = ROPE_BASE ** (-jnp.arange(n_freq, dtype=F32) / n_freq)
    ang = jnp.stack([row[:, None] * inv, col[:, None] * inv], axis=1)
    return jnp.cos(ang), jnp.sin(ang)

def apply_axial_rope(x, cos, sin):
    sh = x.shape
    xr = x.astype(F32).reshape(sh[:-1] + (2, 2, A_DQK // 4))
    xa, xb = xr[..., 0, :], xr[..., 1, :]
    cs, sn = cos[:, None, None], sin[:, None, None]
    out = jnp.stack([xa * cs - xb * sn, xb * cs + xa * sn], axis=-2)
    return out.reshape(sh).astype(x.dtype)

def diff_softmax(q, k, v, lam):
    s = jnp.einsum('bhqcd,bhkcd->bhcqk', q.astype(F32), k.astype(F32)) * (A_DQK ** -0.5)
    p = jax.nn.softmax(s, axis=-1)
    a = p[:, :, 0] - lam * p[:, :, 1]
    return jnp.einsum('bhqk,bhkv->bhqv', a, v.astype(F32))

def diff_attention_branch(p, pc, qk_gain, lam_vec, subln_w, lambda_init, need_ctx):
    def split_heads(pp):
        b_, l_, _ = pp.shape
        q = pp[..., OFF_AQ:OFF_AK].reshape(b_, l_, A_HEADS, 2, A_DQK)
        k = pp[..., OFF_AK:OFF_AV].reshape(b_, l_, A_HEADS, 2, A_DQK)
        v = pp[..., OFF_AV:OFF_HY].reshape(b_, l_, A_HEADS, A_DV)
        return rmsnorm(q, qk_gain[0]), rmsnorm(k, qk_gain[1]), v

    b, l = p.shape[:2]
    q, k, v = split_heads(p)
    qc, kc, vc = split_heads(pc)
    cos, sin = axial_rope_tables(l)
    q = apply_axial_rope(q, cos, sin)
    k = apply_axial_rope(k, cos, sin)
    lf = lam_vec.astype(F32)
    lam = jnp.exp(jnp.sum(lf[0] * lf[1])) - jnp.exp(jnp.sum(lf[2] * lf[3])) + lambda_init
    kc_t = kc.transpose(0, 2, 1, 3, 4)
    vc_t = vc.transpose(0, 2, 1, 3)
    k_all = jnp.concatenate([kc_t, k.transpose(0, 2, 1, 3, 4)], axis=2)
    v_all = jnp.concatenate([vc_t, v.transpose(0, 2, 1, 3)], axis=2)
    n_blk = l // A_QBLOCK
    qb = q.reshape(b, n_blk, A_QBLOCK, A_HEADS, 2, A_DQK).transpose(1, 0, 3, 2, 4, 5)
    o = lax.map(lambda blk: diff_softmax(blk, k_all, v_all, lam), qb)
    o = o.transpose(1, 0, 3, 2, 4).reshape(b, l, A_HEADS, A_DV)

    def finish(oo):
        b_, l_ = oo.shape[:2]
        y = rmsnorm(oo, subln_w) * (1.0 - lambda_init)
        return y.reshape(b_, l_, A_HEADS * A_DV).astype(p.dtype)

    y = finish(o)
    yc = None
    if need_ctx:
        oc = diff_softmax(qc.transpose(0, 2, 1, 3, 4), kc_t, vc_t, lam).transpose(0, 2, 1, 3)
        yc = finish(oc)
    return y, yc

def hyena_filter_spectra(length, w1, b1, freq, w2, b2, w3):
    t = jnp.linspace(0.0, 1.0, length, dtype=F32)[:, None]
    w = 2.0 * math.pi * jnp.arange(length, dtype=F32)[:, None] / length
    bands = jnp.linspace(1e-4, HY_BANDS - 1, HY_BANDS, dtype=F32)[None]
    feats = jnp.concatenate([t, jnp.cos(bands * w), -jnp.sin(bands * w)], axis=-1)
    hdn = jnp.sin(freq[0].astype(F32) * (feats @ w1.astype(F32) + b1.astype(F32)))
    hdn = jnp.sin(freq[1].astype(F32) * (hdn @ w2.astype(F32) + b2.astype(F32)))
    h = (hdn @ w3.astype(F32)).reshape(length, HY_ORDER, 2, HY_W)
    deltas = jnp.abs(jnp.linspace(HY_MIN_DECAY, HY_MAX_DECAY, HY_W, dtype=F32))
    h = h * jnp.exp(-t[:, :, None, None] * deltas)
    taps = jnp.concatenate([h[:, :, 0], jnp.zeros((1, HY_ORDER, HY_W), F32), h[:0:-1, :, 1]], axis=0)
    taps = taps / jnp.sum(jnp.abs(taps), axis=0, keepdims=True)
    return jnp.fft.rfft(taps, n=2 * length, axis=0)

def long_conv(z, kf, bias):
    length = z.shape[1]
    zf = jnp.fft.rfft(z, n=2 * length, axis=1)
    return jnp.fft.irfft(zf * kf, n=2 * length, axis=1)[:, :length] + bias * z

def hyena_branch(pp, conv_w, w1, b1, freq, w2, b2, w3, bias):
    length = pp.shape[1]
    u = centred_conv(pp[..., OFF_HY:OFF_FN], conv_w).astype(F32)
    parts = jnp.split(u, HY_ORDER + 1, axis=-1)
    kf = hyena_filter_spectra(length, w1, b1, freq, w2, b2, w3)
    z = parts[-1]
    for n in range(HY_ORDER):
        z = parts[n] * long_conv(z, kf[:, n], bias[n].astype(F32))
    return z.astype(pp.dtype)

def fourier_branch(pp):
    b, l, _ = pp.shape
    u = pp[..., OFF_FN:OFF_DN].astype(F32).reshape(b, l, FN_GROUPS, FN_W // FN_GROUPS)
    y = jnp.fft.fft2(u, axes=(1, 3), norm='ortho').real
    return y.reshape(b, l, FN_W).astype(pp.dtype)

def gated_delta_chunked(q, k, v, g, beta, s0):
    b, h, l, dk = q.shape
    dv = v.shape[-1]
    cs = DN_CHUNK
    n = l // cs
    q = (q * dk ** -0.5).reshape(b, h, n, cs, dk)
    k = k.reshape(b, h, n, cs, dk)
    v = v.reshape(b, h, n, cs, dv)
    beta = beta.reshape(b, h, n, cs)
    gc = jnp.cumsum(g.reshape(b, h, n, cs), axis=-1)
    idx = jnp.arange(cs)
    incl = idx[:, None] >= idx[None, :]
    strict = idx[:, None] > idx[None, :]
    diff = gc[..., :, None] - gc[..., None, :]
    decay = jnp.where(incl, jnp.exp(jnp.where(incl, diff, 0.0)), 0.0)
    kb = k * beta[..., None]
    a_mat = jnp.where(strict, jnp.einsum('bhncd,bhnsd->bhncs', kb, k) * decay, 0.0)
    eye = jnp.eye(cs, dtype=q.dtype)
    t_mat = lax.linalg.triangular_solve(a_mat + eye, jnp.broadcast_to(eye, a_mat.shape),
                                        left_side=True, lower=True, unit_diagonal=True)
    u_c = t_mat @ (v * beta[..., None])
    w_c = t_mat @ (kb * jnp.exp(gc)[..., None])
    intra = jnp.where(incl, jnp.einsum('bhncd,bhnsd->bhncs', q, k) * decay, 0.0)
    q_dec = q * jnp.exp(gc)[..., None]
    k_dec = k * jnp.exp(gc[..., -1:] - gc)[..., None]
    g_last = jnp.exp(gc[..., -1])
    xs = (jnp.moveaxis(u_c, 2, 0), jnp.moveaxis(w_c, 2, 0), jnp.moveaxis(intra, 2, 0),
          jnp.moveaxis(q_dec, 2, 0), jnp.moveaxis(k_dec, 2, 0), jnp.moveaxis(g_last, 2, 0))

    def step(s, inp):
        u_i, w_i, a_i, qd_i, kd_i, gl_i = inp
        v_new = u_i - jnp.einsum('bhck,bhkv->bhcv', w_i, s)
        o_i = jnp.einsum('bhck,bhkv->bhcv', qd_i, s) + jnp.einsum('bhcs,bhsv->bhcv', a_i, v_new)
        s = s * gl_i[..., None, None] + jnp.einsum('bhck,bhcv->bhkv', kd_i, v_new)
        return s, o_i

    s_fin, o = lax.scan(step, s0, xs)
    o = jnp.moveaxis(o, 0, 2).reshape(b, h, l, dv)
    return o, s_fin

def _flip(t, rev):
    return jnp.flip(t, axis=2) if rev else t

def deltanet_branch(p, pc, conv_w, a_log, dt_bias, norm_w, need_ctx):
    def prep(pp):
        b_, l_, _ = pp.shape
        qkv = jax.nn.silu(centred_conv(pp[..., OFF_DN:OFF_DZ], conv_w).astype(F32))
        q, k, v = jnp.split(qkv, [DN_HEADS * DN_DK, 2 * DN_HEADS * DN_DK], axis=-1)
        q = l2norm(q.reshape(b_, l_, DN_HEADS, DN_DK)).transpose(0, 2, 1, 3)
        k = l2norm(k.reshape(b_, l_, DN_HEADS, DN_DK)).transpose(0, 2, 1, 3)
        v = v.reshape(b_, l_, DN_HEADS, DN_DV).transpose(0, 2, 1, 3)
        a = pp[..., OFF_DA:OFF_DB].astype(F32).reshape(b_, l_, 2, DN_HEADS)
        bt = pp[..., OFF_DB:N_IN].astype(F32).reshape(b_, l_, 2, DN_HEADS)
        g = -jnp.exp(a_log.astype(F32)) * jax.nn.softplus(a + dt_bias.astype(F32))
        return q, k, v, g.transpose(2, 0, 3, 1), jax.nn.sigmoid(bt).transpose(2, 0, 3, 1)

    def finish(o, pp):
        b_, l_ = pp.shape[:2]
        z = pp[..., OFF_DZ:OFF_DA].astype(F32).reshape(b_, l_, DN_HEADS, DN_DV)
        y = rmsnorm(o.transpose(0, 2, 1, 3), norm_w) * jax.nn.silu(z)
        return y.reshape(b_, l_, DN_HEADS * DN_DV).astype(pp.dtype)

    qx, kx, vx, gx, bx = prep(p)
    qc, kc, vc, gcc, bcc = prep(pc)
    s0 = jnp.zeros((p.shape[0], DN_HEADS, DN_DK, DN_DV), F32)
    ox = jnp.zeros_like(vx)
    oc = jnp.zeros_like(vc)
    for d in range(2):
        rev = d == 1
        o_c, s_c = gated_delta_chunked(_flip(qc, rev), _flip(kc, rev), _flip(vc, rev),
                                       _flip(gcc[d], rev), _flip(bcc[d], rev), s0)
        o_x, _ = gated_delta_chunked(_flip(qx, rev), _flip(kx, rev), _flip(vx, rev),
                                     _flip(gx[d], rev), _flip(bx[d], rev), s_c)
        ox = ox + _flip(o_x, rev)
        oc = oc + _flip(o_c, rev)
    y = finish(ox, p)
    yc = finish(oc, pc) if need_ctx else None
    return y, yc

def merge_branches(h, ys, w_gate, w_branch, w_o):
    acc = jax.nn.sigmoid(h @ w_gate[0]) * (ys[0] @ w_branch[0])
    for n in range(1, N_BRANCH):
        acc = acc + jax.nn.sigmoid(h @ w_gate[n]) * (ys[n] @ w_branch[n])
    return acc @ w_o

def sq_relu_mlp(h, w1, w2):
    return jnp.square(jax.nn.relu(h @ w1)) @ w2

def setup_inputs(seed: int = 0) -> dict:
    key = jax.random.key(seed)
    ks = jax.random.split(key, 32)

    def nrm(k, shape, scale):
        return jax.random.normal(k, shape, F32) * scale

    L = DEPTH
    dt = jnp.exp(jax.random.uniform(ks[22], (L, 2, DN_HEADS), F32, math.log(1e-3), math.log(1e-1)))
    return {
        'x': nrm(ks[0], (BATCH, SEQ, D_MODEL), 1.0),
        'c': nrm(ks[1], (BATCH, D_MODEL), 1.0),
        'ctx': nrm(ks[2], (BATCH, CTX_LEN, D_MODEL), 1.0),
        'c_ctx': nrm(ks[3], (D_MODEL,), 1.0),
        'w_ada': nrm(ks[4], (L, D_MODEL, 6 * D_MODEL), D_MODEL ** -0.5),
        'b_ada': nrm(ks[5], (L, 6 * D_MODEL), 0.02),
        'norm1': 1.0 + nrm(ks[6], (L, D_MODEL), 0.02),
        'norm2': 1.0 + nrm(ks[7], (L, D_MODEL), 0.02),
        'w_in': nrm(ks[8], (L, D_MODEL, N_IN), D_MODEL ** -0.5),
        'attn_qk_gain': 1.0 + nrm(ks[9], (L, 2, A_DQK), 0.02),
        'attn_lambda': nrm(ks[10], (L, 4, A_DQK), 0.1),
        'attn_subln': 1.0 + nrm(ks[11], (L, A_DV), 0.02),
        'hy_conv': nrm(ks[12], (L, HY_SHORT, (HY_ORDER + 1) * HY_W), HY_SHORT ** -0.5),
        'hy_w1': nrm(ks[13], (L, HY_EMB, HY_HID), HY_EMB ** -0.5),
        'hy_b1': nrm(ks[14], (L, HY_HID), 0.1),
        'hy_freq': 1.0 + nrm(ks[15], (L, 2, HY_HID), 0.05),
        'hy_w2': nrm(ks[16], (L, HY_HID, HY_HID), HY_HID ** -0.5),
        'hy_b2': nrm(ks[17], (L, HY_HID), 0.1),
        'hy_w3': nrm(ks[18], (L, HY_HID, HY_ORDER * 2 * HY_W), HY_HID ** -0.5),
        'hy_bias': nrm(ks[19], (L, HY_ORDER, HY_W), 0.1),
        'dn_conv': nrm(ks[20], (L, DN_SHORT, DN_HEADS * (2 * DN_DK + DN_DV)), DN_SHORT ** -0.5),
        'dn_a_log': jnp.log(jax.random.uniform(ks[21], (L, 2, DN_HEADS), F32, 1.0, 16.0)),
        'dn_dt_bias': dt + jnp.log(-jnp.expm1(-dt)),
        'dn_norm': 1.0 + nrm(ks[23], (L, DN_DV), 0.02),
        'w_gate': nrm(ks[24], (L, N_BRANCH, D_MODEL, D_MODEL), D_MODEL ** -0.5),
        'w_branch': nrm(ks[25], (L, N_BRANCH, BR_W, D_MODEL), BR_W ** -0.5),
        'w_o': nrm(ks[26], (L, D_MODEL, D_MODEL), D_MODEL ** -0.5),
        'w_mlp1': nrm(ks[27], (L, D_MODEL, D_FF), D_MODEL ** -0.5),
        'w_mlp2': nrm(ks[28], (L, D_FF, D_MODEL), D_FF ** -0.5),
    }

def reference(x, c, ctx, c_ctx, w_ada, b_ada, norm1, norm2, w_in, attn_qk_gain, attn_lambda,
              attn_subln, hy_conv, hy_w1, hy_b1, hy_freq, hy_w2, hy_b2, hy_w3, hy_bias,
              dn_conv, dn_a_log, dn_dt_bias, dn_norm, w_gate, w_branch, w_o, w_mlp1, w_mlp2):
    xc = ctx
    for li in range(DEPTH):
        need_ctx = li < DEPTH - 1
        lambda_init = 0.8 - 0.6 * math.exp(-0.3 * li)
        mod = (jax.nn.silu(c) @ w_ada[li] + b_ada[li])[:, None, :]
        mod_c = (jax.nn.silu(c_ctx) @ w_ada[li] + b_ada[li])[None, None, :]
        sh1, sc1, g1, sh2, sc2, g2 = jnp.split(mod, 6, axis=-1)
        sh1c, sc1c, g1c, sh2c, sc2c, g2c = jnp.split(mod_c, 6, axis=-1)

        h = rmsnorm(x, norm1[li]) * (1.0 + sc1) + sh1
        hc = rmsnorm(xc, norm1[li]) * (1.0 + sc1c) + sh1c
        p = h @ w_in[li]
        pc = hc @ w_in[li]

        ya, ya_c = diff_attention_branch(p, pc, attn_qk_gain[li], attn_lambda[li], attn_subln[li],
                                         lambda_init, need_ctx)
        yb = hyena_branch(p, hy_conv[li], hy_w1[li], hy_b1[li], hy_freq[li], hy_w2[li], hy_b2[li],
                          hy_w3[li], hy_bias[li])
        yf = fourier_branch(p)
        yd, yd_c = deltanet_branch(p, pc, dn_conv[li], dn_a_log[li], dn_dt_bias[li], dn_norm[li],
                                   need_ctx)

        x = x + g1 * merge_branches(h, (ya, yb, yf, yd), w_gate[li], w_branch[li], w_o[li])
        h2 = rmsnorm(x, norm2[li]) * (1.0 + sc2) + sh2
        x = x + g2 * sq_relu_mlp(h2, w_mlp1[li], w_mlp2[li])

        if need_ctx:
            yb_c = hyena_branch(pc, hy_conv[li], hy_w1[li], hy_b1[li], hy_freq[li], hy_w2[li],
                                hy_b2[li], hy_w3[li], hy_bias[li])
            yf_c = fourier_branch(pc)
            xc = xc + g1c * merge_branches(hc, (ya_c, yb_c, yf_c, yd_c), w_gate[li], w_branch[li], w_o[li])
            h2c = rmsnorm(xc, norm2[li]) * (1.0 + sc2c) + sh2c
            xc = xc + g2c * sq_relu_mlp(h2c, w_mlp1[li], w_mlp2[li])
    return x


_drawn_inputs = setup_inputs


def setup_inputs(seed=0):
    import zlib

    import numpy as np

    out = dict(_drawn_inputs(seed))
    spreads = {}
    factors = {'norm1': 4.814,
     'norm2': 2.822,
     'attn_qk_gain': 8.0,
     'attn_lambda': 8.0,
     'attn_subln': 60.195,
     'hy_b1': 3.918,
     'hy_freq': 8.0,
     'hy_b2': 3.365,
     'hy_bias': 3.119,
     'dn_norm': 8.0}
    for name, (base, spread) in spreads.items():
        noise = np.random.default_rng([zlib.crc32(name.encode()), seed]).standard_normal(out[name].shape)
        drawn = base * np.exp(spread * noise) if base else spread * noise
        out[name] = jnp.asarray(drawn.astype(out[name].dtype))
    for name, factor in factors.items():
        out[name] = (out[name] * factor).astype(out[name].dtype)
    return out
```

```python
import math
from contextlib import ExitStack

import numpy as np
import concourse.bass as bass
from concourse import mybir

F32 = mybir.dt.float32
ALU = mybir.AluOpType
ACT = mybir.ActivationFunctionType
AX = mybir.AxisListType.X

P = 128
D = 1024
KD = D // P
L = 256
T = 2 * L
NT = T // P
DEPTH = 2
BR_W = 512
HEADS = 4
DFF = 4 * D
N_BRANCH = 4
OFF_AQ, OFF_AK, OFF_AV, OFF_HY, OFF_FN, OFF_DN, OFF_DZ, OFF_DA = 0, 512, 1024, 1536, 3072, 3584, 5120, 5632
EPS = 1e-6
GRID_W = 64
HY_EMB, HY_HID = 33, 64
STRIP = 256
RING = 2
WORK = 6
ADA_RING = 4
ADA_STRIPS = 6 * D // 512
ATT, HY, FN, DN = range(N_BRANCH)

TABLE = {}


def constant_table():
    parts = []

    def put(name, a):
        a = np.asarray(a, np.float64)
        full = np.zeros((P, a.shape[1]))
        full[:a.shape[0]] = a
        start = sum(p.shape[1] for p in parts)
        TABLE[name] = (start, a.shape[1])
        parts.append(full)

    i, j = np.arange(P)[:, None], np.arange(P)[None, :]
    put("ident", i == j)
    put("ones", np.ones((P, P)))
    put("tri0", i <= j)
    put("tri1", i >= j)
    put("far0", np.where(j <= i, 0.0, 1e30))
    put("far1", np.where(j >= i, 0.0, 1e30))
    same = lambda n: i // n == j // n
    put("blk0", same(16) & (j < i))
    put("blk1", same(16) & (j > i))
    for n in (32, 64, 128):
        put(f"off{n}", same(n) & ~same(n // 2))
    t, f = np.arange(L)[:, None], np.arange(L)[None, :]
    ang = np.pi * ((t * f) % (2 * L)) / L
    fwd = np.concatenate([np.cos(ang), -np.sin(ang)], 1)
    fwd[:, L] = (-1.0) ** np.arange(L)
    put("dft", fwd.reshape(2, P, 2 * L).transpose(1, 0, 2).reshape(P, -1))
    inv = np.concatenate([np.cos(ang).T, -np.sin(ang).T], 0) * 2 / (2 * L)
    inv[0] = 1 / (2 * L)
    inv[L] = (-1.0) ** np.arange(L) / (2 * L)
    put("idft", inv.reshape(4, P, L).transpose(1, 0, 2).reshape(P, -1))
    ca = 2 * np.pi * ((i * j) % P) / P
    put("fn_ch", np.concatenate([np.cos(ca), np.sin(ca)], 1) / math.sqrt(P))
    la = 2 * np.pi * ((t * f) % L) / L
    put("fn_tok", (np.concatenate([np.cos(la), -np.sin(la)], 1) / math.sqrt(L)).reshape(2, P, 2 * L)
        .transpose(1, 0, 2).reshape(P, -1))
    inv_f = np.float32(10000.0) ** (-np.arange(16, dtype=np.float32) / np.float32(16))
    pos = np.arange(L, dtype=np.float32)
    rope = np.stack([np.floor(pos / GRID_W)[:, None] * inv_f, (pos % GRID_W)[:, None] * inv_f], 1)
    rope = rope.astype(np.float32).astype(np.float64).reshape(2, P, 32).transpose(1, 0, 2).reshape(P, -1)
    put("cos", np.cos(rope))
    put("sin", np.sin(rope))
    tt = np.linspace(0.0, 1.0, L, dtype=np.float32)[:, None].astype(np.float64)
    w = 2.0 * math.pi * np.arange(L)[:, None] / L
    bands = np.linspace(1e-4, 15, 16)[None]
    put("feats", np.concatenate([tt, np.cos(bands * w), -np.sin(bands * w)], 1).T)
    put("eps", np.full((P, 1), EPS))
    put("one", np.ones((P, 1)))
    deltas = np.abs(np.linspace(math.log(1e-2) / 1.5, math.log(1e-2) / 0.3, BR_W))
    dec = np.exp(-tt * deltas)
    back = dec.copy()
    back[0] = 0.0
    decay = np.stack([dec.reshape(2, P, BR_W), back.reshape(2, P, BR_W)], 2).transpose(1, 0, 2, 3)
    return np.concatenate(parts, 1).astype(np.float32), np.ascontiguousarray(decay.reshape(P, -1)).astype(np.float32)


def build(nc, x, c, ctx, c_ctx, w_ada, b_ada, norm1, norm2, w_in, attn_qk_gain, attn_lambda, attn_subln,
          hy_conv, hy_w1, hy_b1, hy_freq, hy_w2, hy_b2, hy_w3, hy_bias, dn_conv, dn_a_log, dn_dt_bias,
          dn_norm, w_gate, w_branch, w_o, w_mlp1, w_mlp2, table, decay, out):
    es = ExitStack()
    with es:
        def sb(name, shape):
            return es.enter_context(nc.sbuf_tensor(name, shape, F32))

        def sem(name):
            return es.enter_context(nc.semaphore(name))

        tab = sb("tab", [P, table.shape[1]])
        xT = sb("xT", [P, KD, T])
        hT = sb("hT", [P, KD, T])
        y = sb("y", [P, N_BRANCH, HEADS, T])
        ring = sb("ring", [P, RING, KD, STRIP])
        rows = sb("rows", [P, 2, P])
        cols = sb("cols", [P, 2, P])
        cT = sb("cT", [P, KD, 2])
        mod = sb("mod", [P, 48, 2])
        amp = sb("amp", [P, 2, KD, 2])
        rstd = sb("rstd", [P, T])
        tmp = sb("tmp", [P, 2, T])
        wab = sb("wab", [P, KD, 16])
        vecs = sb("vecs", [P, 2 * 64 + P + P + 256 + 8 + 8])
        qkgain, o = vecs[:, 0:128], 128
        subln = vecs[:, 128:256]
        dnnorm = vecs[:, 256:384]
        lamv = vecs[:, 384:640]
        alog = vecs[:, 640:648]
        dtb = vecs[:, 648:656]
        small = sb("small", [P, 1024])
        ARENA = 23600
        arena = sb("arena", [P, ARENA])

        def carve(*shapes):
            at, views = 0, []
            for s in shapes:
                n = int(np.prod(s))
                v = arena[:, at:at + n]
                assert len(s) < 5
                if len(s) == 2:
                    v = v.rearrange("p (a b) -> p a b", a=s[0])
                if len(s) == 3:
                    v = v.rearrange("p (a b c) -> p a b c", a=s[0], b=s[1])
                if len(s) == 4:
                    v = v.rearrange("p (a b c d) -> p a b c d", a=s[0], b=s[1], c=s[2])
                views.append(v)
                at += n
            assert at <= ARENA, at
            return views if len(views) > 1 else views[0]

        def const(name, rows_=P):
            a, n = TABLE[name]
            return tab[0:rows_, a:a + n]

        ident, ones = const("ident"), const("ones")
        eps, one = const("eps"), const("one")

        psum = es.enter_context(nc.psum_tensor("psum", [P, 8, 512], F32))
        unit_bank = [psum[:, b, :] for b in range(2)]
        work_bank = [psum[:, 2 + b, :] for b in range(WORK)]

        dft = const("dft").rearrange("p (t f) -> p t f", t=2)
        idft = const("idft").rearrange("p (k t) -> p k t", k=4)
        ftok = const("fn_tok").rearrange("p (t n) -> p t n", t=2)
        ropes = [const(n).rearrange("p (t a f) -> p t a f", t=2, a=2) for n in ("cos", "sin")]

        stage, adar = carve((NT, D), (ADA_RING, KD, 512))
        SCR = ["dI", "A", "B", "IT", "ITt", "P1", "P2", "P3", "P4", "P5", "U", "Un", "S"]
        qkvT, k_tok, v_tok, scr = carve((12, T), (NT, BR_W), (NT, BR_W), (2, len(SCR), BR_W))
        DS = [{n: scr[:, d, i, :] for i, n in enumerate(SCR)} for d in range(2)]
        dz_tok = scr[:, 0, SCR.index("P1"):SCR.index("P1") + NT, :]
        o_dn = y[:, ATT]
        a_qk, a_v, a_qT, a_kT, a_P, a_aT, a_o, a_sq = carve((2, NT, BR_W), (NT, BR_W), (HEADS, T), (HEADS, T),
                                                           (2, 2, T), (HEADS, T), (NT, BR_W), (2, BR_W))
        AT = {"qk": a_qk, "v": a_v, "qT": a_qT, "kT": a_kT, "P": [a_P[:, 0], a_P[:, 1]], "aT": a_aT, "o": a_o}
        hv = carve((64,), (64,), (L,), (L,), (L,), (2, 2 * BR_W), (2, BR_W), (2, 2, BR_W), (4, BR_W), (4, BR_W),
                   (2, 5, BR_W), (2, T), (NT, 3, BR_W), (BR_W,), (BR_W,))
        HYB = dict(zip(("w1", "w2", "s", "arg", "turns", "w3", "bias", "decay", "z0", "z1", "K", "cb", "u", "inv",
                        "zt"), hv))
        fn_u_, fn_v_ = carve((HEADS, T), (2, HEADS, 2, 2 * P))
        FNB = {"u": fn_u_, "v": fn_v_}
        m_acc, m_a, m_sg = carve((KD, T), (DFF // P, T), (4, T))
        MG = {"acc": m_acc, "a": m_a, "sg": m_sg}
        outs = carve((2, D))

        gv = small[:, 0:32].rearrange("p (t e) -> p t e", t=NT)

        def sm(a, n=32):
            return small[:, a:a + n]

        G_, BETA, GC, EGC, ETOT, EDL, BEG, SC = 0, 32, 64, 160, 192, 224, 256, 288
        O_STAT, QK_STAT, LAM, MAXC, SUMC, HYC = 416, 448, 560, 580, 600, 620
        MT = [[0, 1, 2, 3], [1, 0, 3, 2]]
        COPIES = ["B", "ITt", "A2", "B2", "A4", "B4", "A8", "V0", "Y0", "V1", "Y1", "V2", "Y2", "vn"]
        ROWS_DONE = [7 * 16, 12 * 16]
        HYW = 9 * 16
        TWO_PI = (6.28125, 0.0019340515136718750, 2 * math.pi - 6.28125 - 0.0019340515136718750)
        ROUND = 12582912.0

        def qkn(li):
            return li + 1

        def onum(li, br, i):
            n = NT if li == 0 else 2
            return (0 if li == 0 else 2 * NT) + (0 if br == DN else n) + i + 1

        def att_n(li, i, h):
            return 16 * li + 4 * i + h

        def cv(li, key, blk):
            return 24 * li + (0 if key == "dn" else 12) + blk + 1

        def hyz(li, n, s):
            return 2 * n + s if li == 0 else 4 + n

        def fnn(li, s, g):
            return 4 * s + g if li == 0 else 8 + g

        def yt(li):
            return 20 if li == 0 else 30

        consts_loaded = sem("consts_loaded")
        rows_loaded = sem("rows_loaded")
        x_loaded = sem("x_loaded")
        vecs_loaded = sem("vecs_loaded")
        hyw_loaded = sem("hyw_loaded")
        ada_loaded = [sem(f"ada_loaded{i}") for i in range(ADA_RING)]
        ada_used = sem("ada_used")
        strip_loaded = [sem(f"strip_loaded{i}") for i in range(RING)]
        unit_done = sem("unit_done")
        unit_free = [sem(f"unit_free{b}") for b in range(2)]
        filled = sem("filled")
        work_free = [sem(f"work_free{b}") for b in range(WORK)]
        act_step, dve_step, pool_step = sem("act_step"), sem("dve_step"), sem("pool_step")
        act_left, dve_left, pool_left = sem("act_left"), sem("dve_left"), sem("pool_left")
        names = ("cols_ready cT_ready mod_ready sq_ready sum_taken rstd_ready h_ready x_ready x_added gate_cols "
                 "g_ready decays_ready block_conv block_silu block_sq block_rstd block_normed block_tok "
                 "token_copied seg_ready o_normed y_turned stat_ready stat_root qk_ready qkT_ready max_ready "
                 "exp_ready a_ready aT_ready o_copied hyf_arg hyf_sin hyf_taps z_ready zf_ready hy_u fn_u fn_v "
                 "sg_ready mul_done acc_added relu_ready mlp_ready out_ready out_stored").split()
        S = {n: sem(n) for n in names}
        dnames = ("trig_ready far_ready dI_ready A_ready IT_ready blk_ready U_ready aoff_ready copied vb_ready "
                  "kdec_ready r_ready S_ready o_added").split()
        SD = {n: [sem(f"{n}{d}") for d in range(2)] for n in dnames}

        counts = {}

        def link(eng, ins, s):
            k = (str(eng.engine), s.name)
            counts[k] = counts.get(k, 0) + 1
            ins.then_inc(s, 1)
            eng.wait_ge(s, counts[k])

        def signals(eng, ins, s):
            k = (str(eng.engine), s.name)
            counts[k] = counts.get(k, 0) + 1
            ins.then_inc(s, 1)

        strips = []
        strip_end = []
        first_strip, first_unit, first_mark = {}, {}, {}
        at_unit = at_mark = 0

        def add(key, li, sources, marks, units):
            nonlocal at_unit, at_mark
            first_strip[key, li], first_unit[key, li], first_mark[key, li] = len(strips), at_unit, at_mark
            for src, n in zip(sources, marks):
                strips.append(src)
                at_mark += n
                strip_end.append(at_mark)
            at_unit += units

        def by_columns(w, off, n):
            return [w[:, off + STRIP * s:off + STRIP * (s + 1)].rearrange("(k p) n -> p k n", p=P)
                    for s in range(n // STRIP)]

        PAIRS = [(0, 1), (1,)]
        for li in range(DEPTH):
            np_ = len(PAIRS[li])
            add("dn", li, by_columns(w_in[li], OFF_DN, 1536), [2] * 6, 12)
            add("dz", li, by_columns(w_in[li], OFF_DZ, 512), [np_] * 2, 2 * np_)
            add("aq", li, by_columns(w_in[li], OFF_AQ, 512), [np_] * 2, 2 * np_)
            add("ak", li, by_columns(w_in[li], OFF_AK, 512), [2] * 2, 4)
            add("av", li, by_columns(w_in[li], OFF_AV, 512), [2] * 2, 4)
            add("hy", li, by_columns(w_in[li], OFF_HY, 1536), [2] * 6, 12)
            add("fn", li, by_columns(w_in[li], OFF_FN, 512), [2] * 2, 4)
            add("merge", li, [None] * 24, [2, 2, 4] * 8, 64)
            add("wo", li, by_columns(w_o[li], 0, D), [2] * 4, 8)
            add("mlp1", li, [None] * 16, [2] * 16, 32)
            add("mlp2", li, [None] * 16, [2] * 16, 8)

        def toks(li):
            return slice(0, T) if li < DEPTH - 1 else slice(L, T)

        def tiles(li):
            return range(NT) if li < DEPTH - 1 else range(2, NT)

        def streams(li):
            return range(2) if li < DEPTH - 1 else range(1, 2)

        block = es.enter_context(nc.Block())
        fill_at = {}

        @block.tensor
        def _(pe):
            n_fill = [0]
            n_unit = [0]
            n_strip = [0]

            def fill(key):
                n = n_fill[0]
                n_fill[0] += 1
                fill_at[key] = n
                if n >= WORK:
                    pe.wait_ge(work_free[n % WORK], n // WORK)
                return work_bank[n % WORK]

            def strip():
                n = n_strip[0]
                n_strip[0] += 1
                pe.wait_ge(strip_loaded[n % RING], 16 * (n // RING + 1))
                return ring[:, n % RING]

            def unit():
                n = n_unit[0]
                n_unit[0] += 1
                if n >= 2:
                    pe.wait_ge(unit_free[n % 2], n // 2)
                return unit_bank[n % 2]

            def mm(o_, a, b, start=True, stop=True):
                return nc.tensor.matmul(o_, a, b, start=start, stop=stop)

            def feature_strips(key, li, act, tk):
                assert first_strip[key, li] == n_strip[0] and first_unit[key, li] == n_unit[0]
                n_blocks = {"dn": 12, "fn": 4, "wo": 8}[key]
                for _ in range(n_blocks // 2):
                    w = strip()
                    for cb in range(2):
                        bank = unit()
                        for k in range(KD):
                            m = mm(bank[:, tk], w[:, k, cb * P:(cb + 1) * P], act[:, k, tk], k == 0, k == KD - 1)
                        m.then_inc(unit_done, 1)

            def token_strips(key, li, pairs):
                assert first_strip[key, li] == n_strip[0] and first_unit[key, li] == n_unit[0]
                for _ in range(2):
                    w = strip()
                    for pr in pairs:
                        bank = unit()
                        for mi in range(2):
                            for k in range(KD):
                                m = mm(bank[:, mi * STRIP:(mi + 1) * STRIP],
                                       hT[:, k, (2 * pr + mi) * P:(2 * pr + mi + 1) * P], w[:, k, :],
                                       k == 0, k == KD - 1)
                        m.then_inc(unit_done, 1)

            def turn(bank, src, ids=ident):
                for i, s in enumerate(src):
                    m = nc.tensor.transpose(bank[:, i * P:(i + 1) * P], s, ids)
                return m

            def start_(li):
                pe.wait_ge(rows_loaded, ROWS_DONE[li])
                if li == 0:
                    pe.wait_ge(consts_loaded, 16)
                b = fill(("cols", li))
                nc.tensor.transpose(b[:, 0:100], rows[0:100, 0, :], ident[0:100, 0:100])
                n = 52 if li == 0 else 36
                nc.tensor.transpose(b[:, 128:128 + n], rows[0:n, 1, :], ident[0:n, 0:n]).then_inc(filled, 1)
                if li == 0:
                    pe.wait_ge(x_loaded, 32)
                    for k in range(KD):
                        b = fill(("x", k))
                        turn(b, [stage[:, m, k * P:(k + 1) * P] for m in range(NT)]).then_inc(filled, 1)
                if li == 0:
                    pe.wait_ge(S["cT_ready"], 2)
                b = fill(("mod", li))
                for s in range(ADA_STRIPS):
                    n = li * ADA_STRIPS + s
                    pe.wait_ge(ada_loaded[n % ADA_RING], 16 * (n // ADA_RING + 1))
                    for cb in range(4):
                        for k in range(KD):
                            m = mm(b[:, 8 * s + 2 * cb:8 * s + 2 * cb + 2],
                                   adar[:, n % ADA_RING, k, cb * P:(cb + 1) * P], cT[:, k, :], k == 0, k == KD - 1)
                    if s < ADA_STRIPS - 1:
                        m.then_inc(ada_used, 1)
                m.then_inc(filled, 1)

            def norm(li, which):
                tk = toks(li) if which else slice(0, T)
                n = 2 * li + which
                b = fill(("ms", li, which))
                for k in range(KD):
                    pe.wait_ge(S["sq_ready"], KD * n + k + 1)
                    m = mm(b[:, tk], ones, tmp[:, k % 2, tk], k == 0, k == KD - 1)
                    if k < KD - 1:
                        m.then_inc(S["sum_taken"], 1)
                m.then_inc(filled, 1)

            def dn(li):
                pe.wait_ge(S["h_ready"], 2 * li + 1)
                b = fill(("dab", li))
                for m_ in range(NT):
                    for k in range(KD):
                        m = mm(b[:, 16 * m_:16 * m_ + 16], hT[:, k, m_ * P:(m_ + 1) * P], wab[:, k, :],
                               k == 0, k == KD - 1)
                m.then_inc(filled, 1)
                feature_strips("dn", li, hT, slice(0, T))
                pe.wait_ge(S["g_ready"], li + 1)
                b = fill(("gcum", li))
                bt = b[:, 0:32].rearrange("p (t e) -> p t e", t=NT)
                for d in range(2):
                    mm(bt[:, :, 4 * d:4 * d + 4], const(f"tri{d}"), gv[:, :, 4 * d:4 * d + 4])
                m = mm(b[:, 32:64], ones, small[:, 0:32])
                m.then_inc(filled, 1)
                for blk in range(8):
                    pe.wait_ge(S["block_sq"], li * 8 + blk + 1)
                    b = fill(("ss", li, blk))
                    mm(b, ones, tmp[:, blk % 2, :]).then_inc(filled, 1)
                pe.wait_ge(S["block_normed"], li * 8 + 8)
                for blk in range(4, 12):
                    if blk < 8:
                        pe.wait_ge(S["block_normed"], li * 8 + blk + 1)
                    else:
                        pe.wait_ge(S["block_silu"], li * 12 + blk + 1)
                    b = fill(("tok", li, blk))
                    turn(b, [qkvT[:, blk, m_ * P:(m_ + 1) * P] for m_ in range(NT)]).then_inc(filled, 1)
                for step in range(4):
                    q = li * 4 + step
                    sc = [(d, DS[d], MT[d][step]) for d in range(2)]

                    def heads(b, a, r, lvl=None):
                        for h in range(HEADS):
                            m = mm(b[:, h * P:(h + 1) * P], a(h), r(h))
                        m.then_inc(filled, 1)

                    for d, s, m_ in sc:
                        pe.wait_ge(SD["trig_ready"][d], q + 1)
                        b = fill(("gcb", q, d))
                        mm(b, ones, s["P5"]).then_inc(filled, 1)
                    for nm, ai in (("kk", 4), ("qk", 0)):
                        for d, s, m_ in sc:
                            b = fill((nm, q, d))
                            heads(b, lambda h: qkvT[:, ai + h, m_ * P:(m_ + 1) * P],
                                  lambda h: qkvT[:, 4 + h, m_ * P:(m_ + 1) * P])
                    hs = lambda t: (lambda h: t[:, h * P:(h + 1) * P])
                    for d, s, m_ in sc:
                        pe.wait_ge(SD["A_ready"][d], q + 1)
                        turn(fill(("B", q, d)), [hs(s["A"])(h) for h in range(4)]).then_inc(filled, 1)
                    for d, s, m_ in sc:
                        pe.wait_ge(SD["IT_ready"][d], q + 1)
                        turn(fill(("ITt", q, d)), [hs(s["IT"])(h) for h in range(4)]).then_inc(filled, 1)

                    def prod(nm, a, r, waits):
                        for d, s, m_ in sc:
                            for wn, wk in waits:
                                pe.wait_ge(SD[wn][d], wk)
                            b = fill((nm, q, d))
                            heads(b, hs(s[a]), hs(s[r]))
                    cp = lambda nm: ("copied", q * len(COPIES) + COPIES.index(nm) + 1)
                    prod("A2", "Un", "dI", [("blk_ready", 3 * q + 2)])
                    prod("B2", "dI", "Un", [])
                    prod("A4", "P2", "P1", [cp("B2")])
                    prod("B4", "P1", "P2", [])
                    prod("Ua", "P1", "U", [("blk_ready", 3 * q + 3)])
                    prod("A8", "P4", "P3", [cp("B4")])
                    prod("Ub", "P3", "Un", [("U_ready", 6 * q + 1)])
                    prod("Uc", "P5", "U", [cp("A8"), ("U_ready", 6 * q + 2)])
                    cur, nxt = "Un", "U"
                    for lv in range(3):
                        for d, s, m_ in sc:
                            pe.wait_ge(SD["U_ready"][d], 6 * q + 3 + lv)
                            turn(fill((f"V{lv}", q, d)), [hs(s[cur])(h) for h in range(4)]).then_inc(filled, 1)
                        prod(f"Y{lv}", "dI", cur, [("aoff_ready", 3 * q + lv + 1)])
                        prod(f"M{lv}", "P2", "P4", [cp(f"V{lv}"), cp(f"Y{lv}")])
                        cur, nxt = nxt, cur
                    for d, s, m_ in sc:
                        if step == 0:
                            pe.wait_ge(S["seg_ready"], 2 * (li + 1))
                        else:
                            pe.wait_ge(SD["S_ready"][d], q - li)
                        b = fill(("KS", q, d))
                        heads(b, lambda h: qkvT[:, 4 + h, m_ * P:(m_ + 1) * P], hs(s["S"]))
                        b = fill(("qS", q, d))
                        heads(b, lambda h: qkvT[:, h, m_ * P:(m_ + 1) * P], hs(s["S"]))
                    prod("vn", "U", "P1", [("r_ready", q + 1), ("U_ready", 6 * q + 6)])
                    prod("iv", "ITt", "P3", [cp("vn")])
                    prod("kv", "IT", "P3", [("kdec_ready", q + 1)] ) if step < 3 else None
                token_strips("dz", li, (0, 1) if li < DEPTH - 1 else (1,))
                for i, m_ in enumerate(tiles(li)):
                    pe.wait_ge(S["o_normed"], onum(li, DN, i))
                    b = fill(("yd", li, m_))
                    turn(b, [y[:, ATT, m_, h * P:(h + 1) * P] for h in range(4)]).then_inc(filled, 1)

            def att(li):
                token_strips("aq", li, (0, 1) if li < DEPTH - 1 else (1,))
                token_strips("ak", li, (0, 1))
                token_strips("av", li, (0, 1))
                A = AT
                qi = 0
                for which in range(2):
                    tl = tiles(li) if which == 0 else range(NT)
                    for h in range(HEADS):
                        pe.wait_ge(S["qk_ready"], qkn(li))
                        b = fill(("qkT", li, which, h))
                        for m_ in tl:
                            m = nc.tensor.transpose(b[:, m_ * P:(m_ + 1) * P],
                                                    A["qk"][:, which, m_, h * P:(h + 1) * P], ident)
                        m.then_inc(filled, 1)
                for i, m_ in enumerate(tiles(li)):
                    nk = 2 if m_ < 2 else 4

                    def turned(h):
                        n = att_n(li, i, h)
                        pe.wait_ge(S["a_ready"], n + 1)
                        b = fill(("aT", li, m_, h))
                        turn(b, [A["P"][h % 2][:, 0, kt * P:(kt + 1) * P] for kt in range(nk)]).then_inc(filled, 1)
                    for h in range(HEADS):
                        if i == 0 and h == 0:
                            pe.wait_ge(S["qkT_ready"], 8 * (li + 1))
                        for cc in range(2):
                            b = fill(("s", li, m_, h, cc))
                            sl = slice(64 * cc, 64 * cc + 64)
                            mm(b[:, 0:nk * P], A["qT"][sl, h, m_ * P:(m_ + 1) * P],
                               A["kT"][sl, h, 0:nk * P]).then_inc(filled, 1)
                        if h > 0:
                            turned(h - 1)
                    turned(HEADS - 1)
                    b = fill(("o", li, m_))
                    pe.wait_ge(S["aT_ready"], att_n(li, i, 3) + 1)
                    for h in range(HEADS):
                        for kt in range(nk):
                            m = mm(b[:, h * P:(h + 1) * P], A["aT"][:, h, kt * P:(kt + 1) * P],
                                   A["v"][:, kt, h * P:(h + 1) * P], kt == 0, kt == nk - 1)
                    m.then_inc(filled, 1)
                for i, m_ in enumerate(tiles(li)):
                    pe.wait_ge(S["o_normed"], onum(li, ATT, i))
                    b = fill(("ya", li, m_))
                    turn(b, [A["o"][:, m_, h * P:(h + 1) * P] for h in range(4)]).then_inc(filled, 1)

            def hyena(li):
                H_ = HYB
                pe.wait_ge(hyw_loaded, HYW * (li + 1))
                b = fill(("f1", li))
                mm(b[0:HY_HID, 0:L], H_["w1"][0:HY_EMB, :], const("feats", HY_EMB)).then_inc(filled, 1)
                pe.wait_ge(S["hyf_sin"], 2 * li + 1)
                b = fill(("f2", li))
                mm(b[0:HY_HID, 0:L], H_["w2"][0:HY_HID, :], H_["s"][0:HY_HID, :]).then_inc(filled, 1)
                pe.wait_ge(S["hyf_sin"], 2 * li + 2)
                for n in range(2):
                    for tt in range(2):
                        for dr in range(2):
                            b = fill(("f3", li, n, tt, dr))
                            mm(b, H_["s"][0:HY_HID, tt * P:(tt + 1) * P],
                               H_["w3"][0:HY_HID, n, dr * 512:(dr + 1) * 512]).then_inc(filled, 1)
                    pe.wait_ge(S["hyf_taps"], 2 * li + n + 1)
                    b = fill(("fs", li, n))
                    for tt in range(2):
                        for dr in range(2):
                            m = mm(b, ones, H_["z1"][:, 2 * tt + dr, :], tt + dr == 0, tt + dr == 2)
                    m.then_inc(filled, 1)
                    for fc in range(4):
                        b = fill(("fk", li, n, fc))
                        for tt in range(2):
                            m = mm(b, dft[:, tt, fc * P:(fc + 1) * P], H_["z0"][:, 2 * tt + fc // 2, :],
                                   tt == 0, tt == 1)
                        m.then_inc(filled, 1)
                    b = fill(("fL", li, n))
                    for tt in range(2):
                        m = mm(b, dft[:, tt, 2 * P:3 * P], H_["z0"][:, 2 * tt, :], tt == 0, tt == 1)
                    m.then_inc(filled, 1)
                assert first_strip["hy", li] == n_strip[0]
                tk = toks(li)

                def turned(blk):
                    pe.wait_ge(S["block_conv"], cv(li, "hy", blk))
                    b = fill(("hyu", li, blk))
                    for m_ in tiles(li):
                        m = nc.tensor.transpose(b[:, m_ * P:(m_ + 1) * P], H_["cb"][:, blk % 2, m_ * P:(m_ + 1) * P], ident)
                    m.then_inc(filled, 1)
                for s in range(6):
                    w = strip()
                    for cb in range(2):
                        bank = unit()
                        for k in range(KD):
                            m = mm(bank[:, tk], w[:, k, cb * P:(cb + 1) * P], hT[:, k, tk], k == 0, k == KD - 1)
                        m.then_inc(unit_done, 1)
                        if 2 * s + cb >= 1:
                            turned(2 * s + cb - 1)
                turned(11)
                pe.wait_ge(S["hy_u"], 12 * (li + 1))
                for n in range(2):
                    for s in streams(li):
                        zz = hyz(li, n, s)
                        if n:
                            pe.wait_ge(S["z_ready"], hyz(li, 0, s) + 1)
                        for fc in (0, 2, 1, 3):
                            b = fill(("zf", zz, fc))
                            for tt in range(2):
                                m = mm(b, dft[:, tt, fc * P:(fc + 1) * P], H_["u"][:, 2 * s + tt, 2, :],
                                       tt == 0, tt == 1)
                            m.then_inc(filled, 1)
                        pe.wait_ge(S["zf_ready"], 2 * (zz + 1))
                        for tt in range(2):
                            b = fill(("zt", zz, tt))
                            for i_, fc in enumerate((0, 2, 1, 3)):
                                m = mm(b, idft[:, fc, tt * P:(tt + 1) * P], H_["z0"][:, fc, :], i_ == 0, i_ == 3)
                            m.then_inc(filled, 1)
                for i, m_ in enumerate(tiles(li)):
                    pe.wait_ge(S["z_ready"], hyz(li, 1, m_ // 2) + 1)
                    b = fill(("yh", li, m_))
                    turn(b, [H_["u"][:, m_, 2, h * P:(h + 1) * P] for h in range(4)]).then_inc(filled, 1)

            def fnet(li):
                tk = toks(li)
                feature_strips("fn", li, hT, tk)
                fn = FNB
                fch = const("fn_ch")
                pe.wait_ge(S["fn_u"], 4 * (li + 1))
                i = 0
                for s in streams(li):
                    for g in range(HEADS):
                        b = fill(("fv", li, s, g))
                        for tt in range(2):
                            m = mm(b[:, tt * 256:(tt + 1) * 256], fn["u"][:, g, s * L + tt * P:s * L + (tt + 1) * P], fch)
                        m.then_inc(filled, 1)
                for s in streams(li):
                    for g in range(HEADS):
                        pe.wait_ge(S["fn_v"], fnn(li, s, g) + 1)
                        b = fill(("fy", li, s, g))
                        for i_, (tt, w) in enumerate(((0, 0), (0, 1), (1, 0), (1, 1))):
                            m = mm(b[:, 0:L], fn["v"][:, s, g, tt, w * P:(w + 1) * P],
                                   ftok[:, tt, w * L:(w + 1) * L], i_ == 0, i_ == 3)
                        m.then_inc(filled, 1)

            def merge(li):
                tk = toks(li)
                s0, u0 = first_strip["merge", li], first_unit["merge", li]
                assert s0 == n_strip[0] and u0 == n_unit[0]
                assert s0 % RING == 0 and u0 % 2 == 0
                n_strip[0] += 3 * 8
                n_unit[0] += 8 * 8
                pe.wait_ge(S["y_turned"], yt(li))
                with pe.Fori(0, N_BRANCH) as n:
                    for jj in range(2):
                        for s in range(3):
                            i = 3 * jj + s
                            w = ring[:, i % RING]
                            pe.wait_ge(strip_loaded[i % RING], 16 * ((s0 + i) // RING + 1) + n * (16 * 6 // RING))
                            if s < 2:
                                for cb in range(2):
                                    u = 8 * jj + 2 * s + cb
                                    pe.wait_ge(unit_free[u % 2], (u0 + u) // 2 + n * 8)
                                    for k in range(KD):
                                        m = mm(unit_bank[u % 2][:, tk], w[:, k, cb * P:(cb + 1) * P],
                                               hT[:, k, tk], k == 0, k == KD - 1)
                                    m.then_inc(unit_done, 1)
                            else:
                                wb = w.rearrange("p k n -> p (k n)").rearrange("p (k n) -> p k n", k=4)
                                for cb in range(4):
                                    u = 8 * jj + 4 + cb
                                    pe.wait_ge(unit_free[u % 2], (u0 + u) // 2 + n * 8)
                                    for k in range(4):
                                        m = mm(unit_bank[u % 2][:, tk], wb[:, k, cb * P:(cb + 1) * P],
                                               y[:, bass.ds(n, 1), k, tk].rearrange("p a t -> p (a t)"),
                                               k == 0, k == 3)
                                    m.then_inc(unit_done, 1)

            def tail(li):
                tk = toks(li)
                pe.wait_ge(S["acc_added"], 33 * (li + 1))
                feature_strips("wo", li, MG["acc"], tk)
                norm(li, 1)
                pe.wait_ge(S["h_ready"], 2 * li + 2)
                s0, u0 = first_strip["mlp1", li], first_unit["mlp1", li]
                assert s0 == n_strip[0] and s0 % RING == 0 and u0 == n_unit[0] and u0 % 2 == 0
                n_strip[0] += 16
                n_unit[0] += 32
                with pe.Fori(0, 8) as i:
                    for r in range(RING):
                        pe.wait_ge(strip_loaded[r], 16 * (s0 // RING + 1) + i * 16)
                        for cb in range(2):
                            pe.wait_ge(unit_free[cb], u0 // 2 + r + i * 2)
                            for k in range(KD):
                                m = mm(unit_bank[cb][:, tk], ring[:, r, k, cb * P:(cb + 1) * P], hT[:, k, tk],
                                       k == 0, k == KD - 1)
                            m.then_inc(unit_done, 1)
                s0, u0 = first_strip["mlp2", li], first_unit["mlp2", li]
                assert s0 == n_strip[0] and u0 == n_unit[0]
                n_strip[0] += 16
                n_unit[0] += 8
                pe.wait_ge(S["mlp_ready"], 32 * (li + 1))
                with pe.Fori(0, 4) as i:
                    for cb in range(2):
                        pe.wait_ge(unit_free[cb], u0 // 2 + i)
                    for kc in range(4):
                        pe.wait_ge(strip_loaded[kc % RING], 16 * ((s0 + kc) // RING + 1) + i * (4 // RING * 16))
                        for cb in range(2):
                            for k in range(KD):
                                m = mm(unit_bank[cb][:, tk], ring[:, kc % RING, k, cb * P:(cb + 1) * P],
                                       MG["a"][:, kc * KD + k, tk], kc + k == 0, kc == 3 and k == KD - 1)
                            m.then_inc(unit_done, 1)

            def leave():
                for i in range(4):
                    b = fill(("out", i))
                    pe.wait_ge(S["x_added"], 16 * DEPTH)
                    m_, half = 2 + i // 2, i % 2
                    turn(b, [xT[:, 4 * half + k, m_ * P:(m_ + 1) * P] for k in range(4)]).then_inc(filled, 1)

            for li in range(DEPTH):
                start_(li)
                norm(li, 0)
                dn(li)
                att(li)
                hyena(li)
                fnet(li)
                merge(li)
                tail(li)
            leave()

        def filled_bank(eng, key):
            n = fill_at[key]
            eng.wait_ge(filled, n + 1)
            return work_bank[n % WORK]

        def give_fill(eng, key):
            eng.sem_inc(work_free[fill_at[key] % WORK], 1)

        def unit_bank_of(eng, key, li, i):
            eng.wait_ge(unit_done, first_mark[key, li] + i + 1)
            return unit_bank[(first_unit[key, li] + i) % 2]

        def give_unit(eng, key, li, i):
            eng.sem_inc(unit_free[(first_unit[key, li] + i) % 2], 1)

        left = {"act": act_left, "dve": dve_left, "pool": pool_left}

        def enter(eng, n):
            if n:
                for s_ in left.values():
                    eng.wait_ge(s_, n)

        PHASES = 5

        def ph(li, i):
            return PHASES * li + i

        def bc_heads(v):
            return v.unsqueeze(2).to_broadcast([P, HEADS, P])

        def over_heads(v):
            return v.unsqueeze(1).to_broadcast([P, HEADS, P])

        def hd(v):
            return v.rearrange("p (h n) -> p h n", h=HEADS)

        @block.sync
        def _(sp):
            def load_rows(li):
                if li:
                    sp.wait_ge(filled, fill_at["cols", li - 1] + 1)
                for dst, src in ((rows[0:48, 0, :], b_ada[li]), (rows[48:56, 0, :], norm1[li]),
                                 (rows[56:64, 0, :], norm2[li]),
                                 (rows[64:100, 0, :], hy_conv[li].rearrange("a c -> (a c)")),
                                 (rows[0:36, 1, :], dn_conv[li].rearrange("a c -> (a c)"))):
                    sp.dma_start(dst, src.rearrange("(r c) -> r c", c=P)).then_inc(rows_loaded, 16)
                if li == 0:
                    sp.dma_start(rows[36:44, 1, :], c_ctx.rearrange("(r c) -> r c", c=P)).then_inc(rows_loaded, 16)
                    sp.dma_start(rows[44:52, 1, :], c.rearrange("a (r c) -> (a r) c", c=P)).then_inc(rows_loaded, 16)

            def load_strip(n):
                if n >= RING:
                    sp.wait_ge(unit_done, strip_end[n - RING])
                sp.dma_start(ring[:, n % RING], strips[n]).then_inc(strip_loaded[n % RING], 16)

            for li in range(DEPTH):
                load_rows(li)
                if li == 0:
                    sp.dma_start(tab[:], table).then_inc(consts_loaded, 16)
                    sp.dma_start(stage[:, 0:2, :], ctx[0].rearrange("(m p) d -> p m d", p=P)).then_inc(x_loaded, 16)
                    sp.dma_start(stage[:, 2:4, :], x[0].rearrange("(m p) d -> p m d", p=P)).then_inc(x_loaded, 16)
                enter(sp, ph(li, 0))
                for dst, src in ((qkgain, attn_qk_gain[li].rearrange("a b -> (a b)")), (subln, attn_subln[li]),
                                 (dnnorm, dn_norm[li]), (lamv, attn_lambda[li].rearrange("a b -> (a b)")),
                                 (alog, dn_a_log[li].rearrange("a b -> (a b)")),
                                 (dtb, dn_dt_bias[li].rearrange("a b -> (a b)"))):
                    sp.dma_start(dst, src.unsqueeze(0).to_broadcast([P, src.shape[0]])).then_inc(vecs_loaded, 16)
                sp.dma_start(wab[:], w_in[li, :, OFF_DA:OFF_DA + 16].rearrange("(k p) n -> p k n", p=P))\
                  .then_inc(vecs_loaded, 16)
                for s in range(ADA_STRIPS):
                    n = li * ADA_STRIPS + s
                    if s >= ADA_RING:
                        sp.wait_ge(ada_used, li * (ADA_STRIPS - 1) + s - ADA_RING + 1)
                    sp.dma_start(adar[:, n % ADA_RING],
                                 w_ada[li, :, 512 * s:512 * (s + 1)].rearrange("(k p) n -> p k n", p=P))\
                      .then_inc(ada_loaded[n % ADA_RING], 16)
                for n in range(first_strip["dn", li], first_strip["merge", li]):
                    load_strip(n)
                s0, m0 = first_strip["merge", li], first_mark["merge", li]
                before = [-2, 0, 2, 4, 8, 10]
                with sp.Fori(0, N_BRANCH) as n:
                    for i in range(6):
                        jj, s = i // 3, i % 3
                        sp.wait_ge(unit_done, m0 + before[i] + n * 16)
                        if s < 2:
                            a = (2 * jj + s) * STRIP
                            src = w_gate[li, bass.ds(n, 1), :, a:a + STRIP].rearrange("a (k p) n -> p (a k) n", p=P)
                            dst = ring[:, i % RING]
                        else:
                            src = w_branch[li, bass.ds(n, 1), :, jj * 512:(jj + 1) * 512]\
                                .rearrange("a (k p) n -> p (a k) n", p=P)
                            dst = ring[:, i % RING].rearrange("p k n -> p (k n)").rearrange("p (k n) -> p k n", k=4)
                        sp.dma_start(dst, src).then_inc(strip_loaded[i % RING], 16)
                for n in range(first_strip["wo", li], first_strip["mlp1", li]):
                    load_strip(n)
                m0 = first_mark["mlp1", li]
                with sp.Fori(0, 8) as i:
                    for r in range(RING):
                        sp.wait_ge(unit_done, m0 - 2 + 2 * r + i * 4)
                        src = w_mlp1[li, :, bass.ds(i * (RING * STRIP) + r * STRIP, STRIP)]
                        sp.dma_start(ring[:, r], src.rearrange("(k p) n -> p k n", p=P)).then_inc(strip_loaded[r], 16)
                m0 = first_mark["mlp2", li]
                with sp.Fori(0, 4) as i:
                    for kc in range(4):
                        sp.wait_ge(unit_done, m0 - 2 + 2 * kc + i * 8)
                        src = w_mlp2[li, kc * D:(kc + 1) * D, bass.ds(i * STRIP, STRIP)]
                        sp.dma_start(ring[:, kc % RING], src.rearrange("(k p) n -> p k n", p=P))\
                          .then_inc(strip_loaded[kc % RING], 16)
            sp.wait_ge(S["out_ready"], 4)
            sp.dma_start(out[0].rearrange("(m p) d -> p m d", p=P), outs).then_inc(S["out_stored"], 16)
            sp.wait_ge(S["out_stored"], 16)

        @block.scalar
        def _(act):
            def step(ins, s_=act_step):
                link(act, ins, s_)

            def f(o_, i_, fn, **kw):
                return nc.scalar.activation(o_, i_, fn, **kw)

            def copy(o_, i_):
                return nc.scalar.copy(o_, i_)

            def rsqrt(o_, i_, n, s_, done=None, after=None):
                step(f(o_, i_, ACT.Ln, bias=eps[0:o_.shape[0]], scale=1.0 / n))
                if after:
                    after()
                step(f(o_, o_, ACT.Exp, scale=-0.5), s_)

            def start_(li):
                if li == 0:
                    act.wait_ge(S["cols_ready"], 1)
                    for s_ in range(2):
                        step(f(cT[:, :, s_], cols[:, 1, 36 + 8 * s_:44 + 8 * s_], ACT.Silu), S["cT_ready"])
                    for k in range(KD):
                        b = filled_bank(act, ("x", k))
                        step(copy(xT[:, k, :], b), S["x_ready"])
                        give_fill(act, ("x", k))

            def norm(li, which):
                tk = toks(li) if which else slice(0, T)
                n = 2 * li + which
                act.wait_ge(S["x_added"], 16 * li + 8 * which)
                for k in range(KD):
                    if k >= 2:
                        act.wait_ge(S["sum_taken"], (KD - 1) * n + k - 1)
                    step(f(tmp[:, k % 2, tk], xT[:, k, tk], ACT.Square), S["sq_ready"])
                b = filled_bank(act, ("ms", li, which))
                rsqrt(rstd[:, tk], b[:, tk], D, S["rstd_ready"], after=lambda: give_fill(act, ("ms", li, which)))

            def dn(li):
                act.wait_ge(S["gate_cols"], 2 * li + 1)
                step(f(sm(SC + 32), sm(SC + 32), ACT.Exp))
                step(f(sm(SC + 32), sm(SC + 32), ACT.Ln, bias=one))
                step(f(sm(SC + 96), sm(SC + 96), ACT.Exp, scale=-1.0))
                step(f(sm(HYC, 8), alog, ACT.Exp), S["decays_ready"])
                for blk in range(12):
                    act.wait_ge(S["block_conv"], cv(li, "dn", blk))
                    step(f(qkvT[:, blk, :], qkvT[:, blk, :], ACT.Silu), S["block_silu"])

                def square(blk):
                    step(f(tmp[:, blk % 2, :], qkvT[:, blk, :], ACT.Square), S["block_sq"])
                square(0)
                square(1)
                for blk in range(8):
                    b = filled_bank(act, ("ss", li, blk))
                    rsqrt(tmp[:, blk % 2, :], b, 1, S["block_rstd"], after=lambda: give_fill(act, ("ss", li, blk)))
                    if blk < 6:
                        act.wait_ge(S["block_normed"], 8 * li + blk + 1)
                        square(blk + 2)
                for blk in range(4, 12):
                    b = filled_bank(act, ("tok", li, blk))
                    dst = k_tok if blk < 8 else v_tok
                    step(copy(dst[:, :, (blk % 4) * P:(blk % 4 + 1) * P], hd(b)), S["block_tok"])
                    give_fill(act, ("tok", li, blk))
                act.wait_ge(S["gate_cols"], 2 * li + 2)
                step(f(sm(EGC, 96), sm(GC, 96), ACT.Exp), S["decays_ready"])
                for st in range(4):
                    q = 4 * li + st

                    def cp(nm, dst):
                        for d in range(2):
                            b = filled_bank(act, (nm, q, d))
                            step(copy(DS[d][dst], b), SD["copied"][d])
                            give_fill(act, (nm, q, d))
                    for d in range(2):
                        act.wait_ge(SD["far_ready"][d], q + 1)
                        for h in range(HEADS):
                            v = DS[d]["dI"][:, h * P:(h + 1) * P]
                            col = GC + 8 * MT[d][st] + 4 * d + h
                            step(f(v, v, ACT.Exp, bias=small[:, col:col + 1], scale=-1.0),
                                 SD["dI_ready"][d] if h == 3 else act_step)
                    for nm, dst in (("B", "B"), ("ITt", "ITt"), ("A2", "P1"), ("B2", "P2"), ("A4", "P3"),
                                    ("B4", "P4"), ("A8", "P5"), ("V0", "P2"), ("Y0", "P4"), ("V1", "P2"),
                                    ("Y1", "P4"), ("V2", "P2"), ("Y2", "P4"), ("vn", "P3")):
                        cp(nm, dst)
                for d in range(2):
                    act.wait_ge(SD["o_added"][d], 4 * (li + 1))
                units = 0
                for s_ in range(2):
                    for pr in PAIRS[li]:
                        b = unit_bank_of(act, "dz", li, units)
                        step(f(dz_tok[:, 2 * pr:2 * pr + 2, s_ * STRIP:(s_ + 1) * STRIP],
                               b.rearrange("p (m n) -> p m n", m=2), ACT.Silu), S["token_copied"])
                        give_unit(act, "dz", li, units)
                        units += 1
                stat_root(li, 0, sm(O_STAT, 16), P)
                turned(li, "yd", DN)
                step(copy(small[:, 1000:1001], one), act_left)

            def stat_root(li, i, v, n):
                act.wait_ge(S["stat_ready"], 3 * li + i + 1)
                rsqrt(v, v, n, S["stat_root"])

            def turned(li, nm, br):
                for m_ in tiles(li):
                    b = filled_bank(act, (nm, li, m_))
                    step(copy(y[:, br, :, m_ * P:(m_ + 1) * P], hd(b)), S["y_turned"])
                    give_fill(act, (nm, li, m_))

            def att(li):
                enter(act, ph(li, 1))
                for key, dst in (("aq", a_qk[:, 0]), ("ak", a_qk[:, 1]), ("av", a_v)):
                    u = 0
                    for s_ in range(2):
                        for pr in (PAIRS[li] if key == "aq" else (0, 1)):
                            b = unit_bank_of(act, key, li, u)
                            step(copy(dst[:, 2 * pr:2 * pr + 2, s_ * STRIP:(s_ + 1) * STRIP],
                                      b.rearrange("p (m n) -> p m n", m=2)), S["token_copied"])
                            give_unit(act, key, li, u)
                            u += 1
                act.wait_ge(S["stat_ready"], 3 * li + 2)
                step(f(sm(LAM, 2), sm(LAM, 2), ACT.Exp))
                stat_root(li, 1, sm(QK_STAT, 64), 64)
                for which, dst in ((0, a_qT), (1, a_kT)):
                    tk = toks(li) if which == 0 else slice(0, T)
                    for h in range(HEADS):
                        b = filled_bank(act, ("qkT", li, which, h))
                        step(copy(dst[:, h, tk], b[:, tk]), S["qkT_ready"])
                        give_fill(act, ("qkT", li, which, h))
                for i, m_ in enumerate(tiles(li)):
                    nk = 2 if m_ < 2 else 4

                    def probs_turned(h):
                        b = filled_bank(act, ("aT", li, m_, h))
                        step(copy(a_aT[:, h, 0:nk * P], b[:, 0:nk * P]), S["aT_ready"])
                        give_fill(act, ("aT", li, m_, h))
                    for h in range(HEADS):
                        n = att_n(li, i, h)
                        for cc in range(2):
                            act.wait_ge(S["max_ready"], 2 * n + cc + 1)
                            b = filled_bank(act, ("s", li, m_, h, cc))
                            par = 2 * (n % 2) + cc
                            step(f(a_P[:, h % 2, cc, 0:nk * P], b[:, 0:nk * P], ACT.Exp, scale=0.125,
                                   bias=small[:, MAXC + 8 + par:MAXC + 9 + par],
                                   accum_out=small[:, SUMC + par:SUMC + par + 1]), S["exp_ready"])
                            give_fill(act, ("s", li, m_, h, cc))
                        if h:
                            probs_turned(h - 1)
                    probs_turned(HEADS - 1)
                    b = filled_bank(act, ("o", li, m_))
                    step(copy(a_o[:, m_, :], b), S["o_copied"])
                    give_fill(act, ("o", li, m_))
                stat_root(li, 2, sm(O_STAT, 16), P)
                turned(li, "ya", ATT)
                step(copy(small[:, 1000:1001], one), act_left)

            def hyena(li):
                enter(act, ph(li, 2))
                for dst, src in ((HYB["w1"][0:HY_EMB, :], hy_w1[li]), (HYB["w2"][0:HY_HID, :], hy_w2[li]),
                                 (HYB["w3"][0:HY_HID].rearrange("p a b -> p (a b)"), hy_w3[li]),
                                 (HYB["bias"], hy_bias[li].unsqueeze(0).to_broadcast([P, 2, BR_W])),
                                 (HYB["decay"].rearrange("p a b c -> p (a b c)"), decay),
                                 (small[0:64, HYC:HYC + 1], hy_b1[li].unsqueeze(1)),
                                 (small[0:64, HYC + 1:HYC + 2], hy_b2[li].unsqueeze(1)),
                                 (small[0:64, HYC + 2:HYC + 3], hy_freq[li, 0].unsqueeze(1)),
                                 (small[0:64, HYC + 3:HYC + 4], hy_freq[li, 1].unsqueeze(1))):
                    act.dma_start(dst, src).then_inc(hyw_loaded, 16)
                for i in range(2):
                    act.wait_ge(S["hyf_arg"], 2 * li + i + 1)
                    step(f(HYB["s"][0:HY_HID], HYB["arg"][0:HY_HID], ACT.Sin), S["hyf_sin"])
                for blk in range(12):
                    b = filled_bank(act, ("hyu", li, blk))
                    tl = tiles(li)
                    dst = HYB["u"][:, tl[0]:NT, blk // 4, (blk % 4) * P:(blk % 4 + 1) * P]
                    step(copy(dst, hd(b)[:, tl[0]:NT, :]), S["hy_u"])
                    give_fill(act, ("hyu", li, blk))
                turned(li, "yh", HY)
                step(copy(small[:, 1000:1001], one), act_left)

            def fnet(li):
                tk = toks(li)
                enter(act, ph(li, 3))
                for g in range(HEADS):
                    b = unit_bank_of(act, "fn", li, g)
                    step(copy(fn_u_[:, g, tk], b[:, tk]), S["fn_u"])
                    give_unit(act, "fn", li, g)
                for s_ in streams(li):
                    for g in range(HEADS):
                        b = filled_bank(act, ("fv", li, s_, g))
                        step(copy(fn_v_[:, s_, g].rearrange("p t n -> p (t n)"), b), S["fn_v"])
                        give_fill(act, ("fv", li, s_, g))
                for s_ in streams(li):
                    for g in range(HEADS):
                        b = filled_bank(act, ("fy", li, s_, g))
                        step(copy(y[:, FN, g, s_ * L:(s_ + 1) * L], b[:, 0:L]), S["y_turned"])
                        give_fill(act, ("fy", li, s_, g))
                step(copy(small[:, 1000:1001], one), act_left)

            def merge(li):
                tk = toks(li)
                enter(act, ph(li, 4))
                m0, u0 = first_mark["merge", li], first_unit["merge", li]
                with act.Fori(0, N_BRANCH) as n:
                    for jj in range(2):
                        for g in range(4):
                            if g == 0:
                                act.wait_ge(S["acc_added"], 33 * li + 1 + n * 8 + 4 * jj)
                            act.wait_ge(unit_done, m0 + n * 16 + 8 * jj + g + 1)
                            f(m_sg[:, g, tk], unit_bank[g % 2][:, tk], ACT.Sigmoid).then_inc(S["sg_ready"], 1)
                            act.wait_ge(S["sg_ready"], 32 * li + n * 8 + 4 * jj + g + 1)
                            act.sem_inc(unit_free[g % 2], 1)

            def mlp(li):
                tk = toks(li)
                m0 = first_mark["mlp1", li]
                with act.Fori(0, 8) as i:
                    for g in range(4):
                        act.wait_ge(unit_done, m0 + i * 4 + g + 1)
                        f(m_a[:, bass.ds(i * 4 + g, 1), tk].rearrange("p a t -> p (a t)"), unit_bank[g % 2][:, tk],
                          ACT.Relu).then_inc(S["relu_ready"], 1)
                        act.wait_ge(S["relu_ready"], 32 * li + i * 4 + g + 1)
                        act.sem_inc(unit_free[g % 2], 1)
                step(copy(small[:, 1000:1001], one), act_left)

            for li in range(DEPTH):
                start_(li)
                norm(li, 0)
                dn(li)
                att(li)
                hyena(li)
                fnet(li)
                merge(li)
                norm(li, 1)
                mlp(li)
            enter(act, ph(DEPTH, 0))
            for i in range(4):
                b = filled_bank(act, ("out", i))
                step(copy(outs[:, i // 2, (i % 2) * 512:(i % 2 + 1) * 512], b), S["out_ready"])

        @block.vector
        def _(dve):
            V = nc.vector

            def step(ins, s_=dve_step):
                link(dve, ins, s_)

            def tt(o_, a, b, op, s_=dve_step):
                step(V.tensor_tensor(o_, a, b, op), s_)

            def ts(o_, a, s1, s2, op0, op1=None, s_=dve_step):
                if op1 is None:
                    step(V.tensor_scalar(o_, a, s1, None, op0), s_)
                else:
                    step(V.tensor_scalar(o_, a, s1, s2, op0, op1), s_)

            def stt(o_, a, sc, b, op0, op1, s_=dve_step):
                step(V.scalar_tensor_tensor(o_, a, sc, b, op0, op1), s_)

            def cp(o_, a, s_=dve_step):
                step(V.tensor_copy(o_, a), s_)

            ADD, MUL, SUB, MAX = ALU.add, ALU.mult, ALU.subtract, ALU.max

            def start_(li):
                b = filled_bank(dve, ("cols", li))
                n = 52 if li == 0 else 36
                cp(cols[:, 0, 0:100], b[:, 0:100])
                cp(cols[:, 1, 0:n], b[:, 128:128 + n], S["cols_ready"])
                give_fill(dve, ("cols", li))
                b = filled_bank(dve, ("mod", li))
                tt(mod[:], b[:, 0:96].rearrange("p (f s) -> p f s", s=2),
                   cols[:, 0, 0:48].unsqueeze(2).to_broadcast([P, 48, 2]), ADD)
                give_fill(dve, ("mod", li))
                for w in range(2):
                    stt(amp[:, w], mod[:, 24 * w + 8:24 * w + 16, :], 1.0,
                        cols[:, 0, 48 + 8 * w:56 + 8 * w].unsqueeze(2).to_broadcast([P, KD, 2]), ADD, MUL)

            def norm(li, which):
                dve.wait_ge(S["rstd_ready"], 2 * li + which + 1)
                ss = range(2) if which == 0 else streams(li)
                for k in range(KD):
                    for s_ in ss:
                        sl = slice(s_ * L, (s_ + 1) * L)
                        last = k == KD - 1 and s_ == 1
                        stt(hT[:, k, sl], xT[:, k, sl], amp[:, which, k, s_:s_ + 1], rstd[:, sl], MUL, MUL)
                        ts(hT[:, k, sl], hT[:, k, sl], mod[:, 24 * which + k, s_:s_ + 1], None, ADD,
                           s_=S["h_ready"] if last else dve_step)

            def conv(key, li, blk, dst, base, tk):
                b = unit_bank_of(dve, key, li, blk)
                w = [cols[:, 0 if key == "hy" else 1, base + 12 * i + blk:base + 12 * i + blk + 1] for i in range(3)]
                p3 = b[:, tk].rearrange("p (s t) -> p s t", t=L)
                d3 = dst[:, tk].rearrange("p (s t) -> p s t", t=L)
                ts(d3, p3, w[1], None, MUL)
                stt(d3[:, :, 1:L], p3[:, :, 0:L - 1], w[0], d3[:, :, 1:L], MUL, ADD)
                stt(d3[:, :, 0:L - 1], p3[:, :, 1:L], w[2], d3[:, :, 0:L - 1], MUL, ADD, S["block_conv"])
                give_unit(dve, key, li, blk)

            def t8(v):
                return v.rearrange("p (t e) -> p t e", t=NT)

            def dn(li):
                dve.wait_ge(vecs_loaded, 7 * 16 * (li + 1))
                b = filled_bank(dve, ("dab", li))[:, 0:64].rearrange("p (t e) -> p t e", t=NT)
                tt(t8(sm(SC)), b[:, :, 0:8], dtb.unsqueeze(1).to_broadcast([P, NT, 8]), ADD)
                cp(t8(sm(SC + 96)), b[:, :, 8:16])
                give_fill(dve, ("dab", li))
                ts(sm(SC + 64), sm(SC), 0.0, None, MAX)
                stt(sm(SC + 32), sm(SC), -1.0, sm(SC), MUL, ALU.min, S["gate_cols"])
                for blk in range(12):
                    conv("dn", li, blk, qkvT[:, blk], 0, slice(0, T))
                    if blk == 1:
                        dve.wait_ge(S["decays_ready"], 2 * li + 1)
                        tt(sm(SC), sm(SC + 64), sm(SC + 32), ADD)
                        stt(t8(sm(G_)), t8(sm(SC)), -1.0, small[:, HYC:HYC + 8].unsqueeze(1)
                            .to_broadcast([P, NT, 8]), MUL, MUL)
                        ts(sm(SC + 96), sm(SC + 96), 1.0, None, ADD)
                        step(V.reciprocal(sm(BETA), sm(SC + 96)), S["g_ready"])
                b = filled_bank(dve, ("gcum", li))
                cp(sm(GC, 64), b[:, 0:64])
                give_fill(dve, ("gcum", li))
                tt(sm(GC + 64), sm(GC + 32), sm(GC), SUB, S["gate_cols"])
                for blk in range(8):
                    dve.wait_ge(S["block_rstd"], 8 * li + blk + 1)
                    v = qkvT[:, blk, :]
                    stt(v, v, P ** -0.5 if blk < 4 else 1.0, tmp[:, blk % 2, :], MUL, MUL, S["block_normed"])
                dve.wait_ge(S["decays_ready"], 2 * li + 2)
                tt(sm(BEG), sm(EGC), sm(BETA), MUL)
                for st in range(4):
                    q = 4 * li + st
                    sc = [(d, DS[d], MT[d][st], filled_bank) for d in range(2)]

                    def col4(a, m_, d):
                        return bc_heads(small[:, a + 8 * m_ + 4 * d:a + 8 * m_ + 4 * d + 4])
                    for d in range(2):
                        s_, m_ = DS[d], MT[d][st]
                        b = filled_bank(dve, ("gcb", q, d))
                        tt(hd(s_["dI"]), hd(b), over_heads(const(f"far{d}")), ADD, SD["far_ready"][d])
                        give_fill(dve, ("gcb", q, d))
                    for d in range(2):
                        s_, m_ = DS[d], MT[d][st]
                        dve.wait_ge(SD["dI_ready"][d], q + 1)
                        b = filled_bank(dve, ("kk", q, d))
                        for h in range(HEADS):
                            hs = slice(h * P, (h + 1) * P)
                            col = BETA + 8 * m_ + 4 * d + h
                            stt(s_["A"][:, hs], b[:, hs], small[:, col:col + 1], s_["dI"][:, hs], MUL, MUL,
                                SD["A_ready"][d] if h == 3 else dve_step)
                        give_fill(dve, ("kk", q, d))
                    for d in range(2):
                        s_ = DS[d]
                        b = filled_bank(dve, ("qk", q, d))
                        tt(s_["IT"], b, s_["dI"], MUL, SD["IT_ready"][d])
                        give_fill(dve, ("qk", q, d))
                        tt(hd(s_["dI"]), hd(s_["A"]), over_heads(const(f"blk{d}")), MUL, SD["blk_ready"][d])
                    for d in range(2):
                        s_ = DS[d]
                        dve.wait_ge(SD["copied"][d], 14 * q + 1)
                        tt(hd(s_["Un"]), hd(s_["B"]), over_heads(const(f"blk{1 - d}")), MUL, SD["blk_ready"][d])
                        tt(hd(s_["U"]), over_heads(ident), hd(s_["Un"]), SUB, SD["blk_ready"][d])
                    for nm, cur, nxt, op in (("Ua", "U", "Un", ADD), ("Ub", "Un", "U", ADD), ("Uc", "U", "Un", ADD),
                                             ("M0", "Un", "U", SUB), ("M1", "U", "Un", SUB), ("M2", "Un", "U", SUB)):
                        for d in range(2):
                            s_ = DS[d]
                            b = filled_bank(dve, (nm, q, d))
                            tt(s_[nxt], s_[cur], b, op, SD["U_ready"][d])
                            give_fill(dve, (nm, q, d))
                    for d in range(2):
                        s_, m_ = DS[d], MT[d][st]
                        b = filled_bank(dve, ("KS", q, d))
                        tt(hd(s_["P4"]), hd(b), col4(BEG, m_, d), MUL)
                        give_fill(dve, ("KS", q, d))
                        dve.wait_ge(SD["vb_ready"][d], q + 1)
                        tt(s_["P1"], s_["P1"], s_["P4"], SUB, SD["r_ready"][d])
                        b = filled_bank(dve, ("qS", q, d))
                        tt(hd(s_["P2"]), hd(b), col4(EGC, m_, d), MUL)
                        give_fill(dve, ("qS", q, d))
                    for d in range(2):
                        s_, m_ = DS[d], MT[d][st]
                        if st % 2:
                            tt(s_["P2"], s_["P2"], o_dn[:, m_, :], ADD)
                        b = filled_bank(dve, ("iv", q, d))
                        tt(o_dn[:, m_, :], s_["P2"], b, ADD, SD["o_added"][d])
                        give_fill(dve, ("iv", q, d))
                    if st < 3:
                        for d in range(2):
                            s_, m_ = DS[d], MT[d][st]
                            b = filled_bank(dve, ("kv", q, d))
                            tt(hd(s_["S"]), hd(s_["S"]), col4(ETOT, m_, d), MUL)
                            tt(s_["S"], s_["S"], b, ADD, SD["S_ready"][d])
                            give_fill(dve, ("kv", q, d))
                token_norm(li, 0, o_dn, dnnorm, DN, DS[1]["A"])
                cp(small[:, 1001:1002], one, dve_left)

            def token_norm(li, i, o_, gain, br, scratch):
                for m_ in tiles(li):
                    tt(scratch, o_[:, m_, :], o_[:, m_, :], MUL)
                    step(V.tensor_reduce(small[:, O_STAT + 4 * m_:O_STAT + 4 * m_ + 4], hd(scratch), AX, ADD),
                         S["stat_ready"] if m_ == NT - 1 else dve_step)
                dve.wait_ge(S["stat_root"], 3 * li + i + 1)
                if br == DN:
                    dve.wait_ge(S["token_copied"], (0 if li == 0 else 16) + (4 if li == 0 else 2))
                for m_ in tiles(li):
                    v = hd(o_[:, m_, :])
                    tt(v, v, bc_heads(small[:, O_STAT + 4 * m_:O_STAT + 4 * m_ + 4]), MUL)
                    if br == DN:
                        tt(o_[:, m_, :], o_[:, m_, :], dz_tok[:, m_, :], MUL)
                    tt(v, v, over_heads(gain), MUL, S["o_normed"])

            def att(li):
                lam_init = 0.8 - 0.6 * math.exp(-0.3 * li)
                enter(dve, ph(li, 1))
                l4 = lamv.rearrange("p (a b n) -> p a b n", a=2, b=2)
                sq = a_sq[:, 0, 0:128].rearrange("p (a n) -> p a n", a=2)
                tt(sq, l4[:, :, 0, :], l4[:, :, 1, :], MUL)
                step(V.tensor_reduce(sm(LAM, 2), sq, AX, ADD))
                ts(subln, subln, 1.0 - lam_init, None, MUL)
                dve.wait_ge(S["token_copied"], 12 if li == 0 else 16 + 8)
                for which in range(2):
                    tl = tiles(li) if which == 0 else range(NT)
                    for m_ in tl:
                        v = a_qk[:, which, m_, :]
                        tt(a_sq[:, 0, :], v, v, MUL)
                        c0 = QK_STAT + 8 * (4 * which + m_)
                        step(V.tensor_reduce(small[:, c0:c0 + 8], a_sq[:, 0, :].rearrange("p (g n) -> p g n", g=8),
                                             AX, ADD), S["stat_ready"] if (which, m_) == (1, NT - 1) else dve_step)
                dve.wait_ge(S["stat_root"], 3 * li + 2)
                tt(sm(LAM + 2, 1), sm(LAM + 1, 1), sm(LAM, 1), SUB)
                ts(sm(LAM + 3, 1), sm(LAM + 2, 1), -lam_init, None, ADD)
                for which in range(2):
                    tl = tiles(li) if which == 0 else range(NT)
                    for m_ in tl:
                        v = a_qk[:, which, m_, :].rearrange("p (g n) -> p g n", g=8)
                        c0 = QK_STAT + 8 * (4 * which + m_)
                        tt(v, v, small[:, c0:c0 + 8].unsqueeze(2).to_broadcast([P, 8, 64]), MUL)
                        last = (which, m_) == (1, NT - 1)
                        tt(v, v, qkgain[:, 64 * which:64 * which + 64].unsqueeze(1).to_broadcast([P, 8, 64]), MUL)
                        if m_ >= 2:
                            x5 = a_qk[:, which, m_, :].rearrange("p (g a h f) -> p g a h f", g=8, a=2, h=2)
                            xa, xb = x5[:, :, :, 0, :], x5[:, :, :, 1, :]
                            cs, sn = (r[:, m_ - 2].unsqueeze(1).to_broadcast([P, 8, 2, 16]) for r in ropes)
                            q4 = [a_sq[:, i // 2, (i % 2) * 256:(i % 2 + 1) * 256]
                                  .rearrange("p (g a f) -> p g a f", g=8, a=2) for i in range(4)]
                            tt(q4[0], xa, cs, MUL)
                            tt(q4[1], xb, sn, MUL)
                            tt(q4[2], xb, cs, MUL)
                            tt(q4[3], xa, sn, MUL)
                            tt(xa, q4[0], q4[1], SUB)
                            tt(xb, q4[2], q4[3], ADD, S["qk_ready"] if last else dve_step)
                for i, m_ in enumerate(tiles(li)):
                    nk = 2 if m_ < 2 else 4

                    def combine(h):
                        n = att_n(li, i, h)
                        par = n % 2
                        dve.wait_ge(S["exp_ready"], 2 * n + 2)
                        r = small[:, SUMC + 2 * par:SUMC + 2 * par + 2]
                        step(V.reciprocal(r, r))
                        tt(r[:, 1:2], r[:, 1:2], sm(LAM + 3, 1), MUL)
                        p = a_P[:, h % 2]
                        ks = slice(0, nk * P)
                        ts(p[:, 0, ks], p[:, 0, ks], r[:, 0:1], None, MUL)
                        stt(p[:, 0, ks], p[:, 1, ks], r[:, 1:2], p[:, 0, ks], MUL, ADD, S["a_ready"])
                    for h in range(HEADS):
                        n = att_n(li, i, h)
                        for cc in range(2):
                            par = 2 * (n % 2) + cc
                            b = filled_bank(dve, ("s", li, m_, h, cc))
                            step(V.tensor_reduce(small[:, MAXC + par:MAXC + par + 1], b[:, 0:nk * P], AX, MAX))
                            ts(small[:, MAXC + 8 + par:MAXC + 9 + par], small[:, MAXC + par:MAXC + par + 1], -0.125,
                               None, MUL, s_=S["max_ready"])
                        if h:
                            combine(h - 1)
                    combine(HEADS - 1)
                dve.wait_ge(S["o_copied"], 4 if li == 0 else 6)
                token_norm(li, 2, a_o, subln, ATT, a_sq[:, 0, :])
                cp(small[:, 1001:1002], one, dve_left)

            def hyena(li):
                enter(dve, ph(li, 2))
                H_ = HYB
                for i in range(2):
                    b = filled_bank(dve, (f"f{i + 1}", li))
                    dve.wait_ge(hyw_loaded, HYW * (li + 1))
                    a = H_["arg"][0:HY_HID]
                    k = H_["turns"][0:HY_HID]
                    ts(a, b[0:HY_HID, 0:L], small[0:64, HYC + i:HYC + i + 1], small[0:64, HYC + 2 + i:HYC + 3 + i], ADD, MUL)
                    give_fill(dve, (f"f{i + 1}", li))
                    ts(k, a, 1 / (2 * math.pi), None, MUL)
                    ts(k, k, ROUND, None, ADD)
                    ts(k, k, ROUND, None, SUB)
                    for part in TWO_PI:
                        stt(a, k, -part, a, MUL, ADD)
                    ts(a, a, -3.1415925, 3.1415925, MAX, ALU.min, s_=S["hyf_arg"])
                for n in range(2):
                    K = H_["K"][:, n]
                    for t_ in range(2):
                        for dr in range(2):
                            b = filled_bank(dve, ("f3", li, n, t_, dr))
                            tt(H_["z1"][:, 2 * t_ + dr, :], b, H_["decay"][:, t_, dr, :], MUL)
                            give_fill(dve, ("f3", li, n, t_, dr))
                    for t_ in range(2):
                        f0, f1 = H_["z1"][:, 2 * t_, :], H_["z1"][:, 2 * t_ + 1, :]
                        tt(H_["z0"][:, 2 * t_, :], f0, f1, ADD)
                        tt(H_["z0"][:, 2 * t_ + 1, :], f0, f1, SUB)
                    z1f = H_["z1"].rearrange("p a b -> p (a b)")
                    stt(z1f, z1f, -1.0, z1f, MUL, MAX, S["hyf_taps"])
                    b = filled_bank(dve, ("fs", li, n))
                    step(V.reciprocal(H_["inv"], b))
                    give_fill(dve, ("fs", li, n))
                    for fc in range(4):
                        b = filled_bank(dve, ("fk", li, n, fc))
                        tt(K[:, fc, :], b, H_["inv"], MUL)
                        give_fill(dve, ("fk", li, n, fc))
                    b = filled_bank(dve, ("fL", li, n))
                    cp(K[:, 4, :], K[:, 0, :])
                    tt(K[0:1, 4, :], b[0:1, :], H_["inv"][0:1, :], MUL)
                    give_fill(dve, ("fL", li, n))
                    step(V.memset(K[0:1, 2, :], 0.0))
                for blk in range(12):
                    if blk >= 2:
                        dve.wait_ge(filled, fill_at["hyu", li, blk - 2] + 1)
                    conv("hy", li, blk, H_["cb"][:, blk % 2], 64, toks(li))
                dve.wait_ge(S["hy_u"], 12 * (li + 1))
                for n in range(2):
                    K = H_["K"][:, n]
                    for s_ in streams(li):
                        zz = hyz(li, n, s_)
                        z0, z1 = H_["z0"], H_["z1"]
                        for re, kr, ki, kr2 in ((0, 0, 2, 4), (1, 1, 3, 1)):
                            br, bi = (filled_bank(dve, ("zf", zz, re)), filled_bank(dve, ("zf", zz, re + 2)))
                            tt(z0[:, re, :], br, K[:, kr, :], MUL)
                            tt(z0[:, re + 2, :], br, K[:, ki, :], MUL)
                            give_fill(dve, ("zf", zz, re))
                            tt(z1[:, re, :], bi, K[:, ki, :], MUL)
                            tt(z1[:, re + 2, :], bi, K[:, kr2, :], MUL)
                            give_fill(dve, ("zf", zz, re + 2))
                            tt(z0[:, re, :], z0[:, re, :], z1[:, re, :], SUB)
                            tt(z0[:, re + 2, :], z0[:, re + 2, :], z1[:, re + 2, :], ADD, S["zf_ready"])
                        for t_ in range(2):
                            u = H_["u"][:, 2 * s_ + t_]
                            tt(H_["zt"], u[:, 2, :], H_["bias"][:, n, :], MUL)
                            b = filled_bank(dve, ("zt", zz, t_))
                            tt(H_["zt"], H_["zt"], b, ADD)
                            give_fill(dve, ("zt", zz, t_))
                            tt(u[:, 2, :], H_["zt"], u[:, n, :], MUL, S["z_ready"] if t_ else dve_step)
                cp(small[:, 1001:1002], one, dve_left)

            def merge(li):
                tk = toks(li)
                m0 = first_mark["merge", li]
                cp(small[:, 1001:1002], one, dve_left)
                enter(dve, ph(li, 4))
                step(V.memset(m_acc, 0.0), S["acc_added"])
                with dve.Fori(0, N_BRANCH) as n:
                    for jj in range(2):
                        for g in range(4):
                            i = 4 * jj + g
                            dve.wait_ge(unit_done, m0 + n * 16 + 8 * jj + 4 + g + 1)
                            dve.wait_ge(S["sg_ready"], 32 * li + n * 8 + 4 * jj + g + 1)
                            V.tensor_tensor(tmp[:, g % 2, tk], unit_bank[g % 2][:, tk], m_sg[:, g, tk], MUL)\
                             .then_inc(S["mul_done"], 1)
                            dve.wait_ge(S["mul_done"], 32 * li + n * 8 + i + 1)
                            dve.sem_inc(unit_free[g % 2], 1)
                            V.tensor_tensor(m_acc[:, i, tk], m_acc[:, i, tk], tmp[:, g % 2, tk], ADD)\
                             .then_inc(S["acc_added"], 1)
                            dve.wait_ge(S["acc_added"], 33 * li + 1 + n * 8 + i + 1)

            def residual(key, li, gate):
                for blk in range(KD):
                    if key == "wo":
                        b = unit_bank_of(dve, key, li, blk)
                    else:
                        dve.wait_ge(unit_done, first_mark[key, li] + 8 * (blk // 2) + 7 + blk % 2)
                        b = unit_bank[blk % 2]
                    for s_ in streams(li):
                        sl = slice(s_ * L, (s_ + 1) * L)
                        stt(xT[:, blk, sl], b[:, sl], mod[:, gate + blk, s_:s_ + 1], xT[:, blk, sl], MUL, ADD,
                            S["x_added"] if s_ == 1 else dve_step)
                    dve.sem_inc(unit_free[blk % 2], 1)

            def mlp(li):
                tk = toks(li)
                with dve.Fori(0, 8) as i:
                    for g in range(4):
                        dve.wait_ge(S["relu_ready"], 32 * li + i * 4 + g + 1)
                        v = m_a[:, bass.ds(i * 4 + g, 1), tk].rearrange("p a t -> p (a t)")
                        V.tensor_tensor(v, v, v, MUL).then_inc(S["mlp_ready"], 1)
                residual("mlp2", li, 40)
                cp(small[:, 1001:1002], one, dve_left)

            for li in range(DEPTH):
                start_(li)
                norm(li, 0)
                dn(li)
                att(li)
                hyena(li)
                merge(li)
                residual("wo", li, 16)
                norm(li, 1)
                mlp(li)

        @block.gpsimd
        def _(pool):
            G = nc.gpsimd

            def step(ins, s_=pool_step):
                link(pool, ins, s_)

            def dn(li):
                pool.wait_ge(S["g_ready"], li + 1)
                for d in range(2):
                    step(G.memset(DS[d]["S"], 0.0), S["seg_ready"])
                for st in range(4):
                    q = 4 * li + st

                    def col4(a, m_, d):
                        return bc_heads(small[:, a + 8 * m_ + 4 * d:a + 8 * m_ + 4 * d + 4])
                    for d in range(2):
                        m_ = MT[d][st]
                        if st:
                            pool.wait_ge(SD["S_ready"][d], q - li)
                        step(G.tensor_tensor(hd(DS[d]["P5"]), over_heads(const(f"tri{d}")), col4(G_, m_, d), ALU.mult),
                             SD["trig_ready"][d])
                    if st == 0:
                        pool.wait_ge(S["decays_ready"], 2 * (li + 1))
                        pool.wait_ge(S["block_tok"], 8 * (li + 1))
                    for lv, cp_ in ((0, 4), (1, 9), (2, 11)):
                        for d in range(2):
                            m_, s_ = MT[d][st], DS[d]
                            pool.wait_ge(SD["copied"][d], 14 * q + cp_)
                            pool.wait_ge(SD["A_ready"][d], q + 1)
                            step(G.tensor_tensor(hd(s_["dI"]), hd(s_["A"]), over_heads(const(f"off{32 << lv}")),
                                                 ALU.mult), SD["aoff_ready"][d])
                            if lv == 0:
                                step(G.tensor_tensor(hd(s_["IT"]), hd(k_tok[:, m_, :]), col4(EDL, m_, d), ALU.mult),
                                     SD["kdec_ready"][d])
                                pool.wait_ge(SD["U_ready"][d], 6 * q + 1)
                                step(G.tensor_tensor(hd(s_["P1"]), hd(v_tok[:, m_, :]), col4(BETA, m_, d), ALU.mult),
                                     SD["vb_ready"][d])

            for li in range(DEPTH):
                enter(pool, ph(li, 0))
                dn(li)
                for i in range(PHASES):
                    step(G.memset(small[:, 1002:1003], 0.0), pool_left)
    return nc


_INS = ["x", "c", "ctx", "c_ctx", "w_ada", "b_ada", "norm1", "norm2", "w_in", "attn_qk_gain", "attn_lambda",
        "attn_subln", "hy_conv", "hy_w1", "hy_b1", "hy_freq", "hy_w2", "hy_b2", "hy_w3", "hy_bias", "dn_conv",
        "dn_a_log", "dn_dt_bias", "dn_norm", "w_gate", "w_branch", "w_o", "w_mlp1", "w_mlp2"]
_OUTS = [((1, L, D), "float32")]


def kernel(**inputs):
    import numpy as _np
    import concourse.bacc as _bacc
    from concourse import mybir as _mybir
    from concourse.bass_utils import run_bass_kernel_spmd as _run

    nc = _bacc.Bacc("TRN2", target_bir_lowering=False, num_devices=1)
    table, decay = constant_table()
    arrays, args = {}, []
    for name in _INS + ["table", "decay"]:
        a = _np.ascontiguousarray({"table": table, "decay": decay}[name] if name in ("table", "decay") else inputs[name])
        arrays[f"in_{name}_dram"] = a
        args.append(nc.dram_tensor(f"in_{name}_dram", a.shape, _mybir.dt.from_np(a.dtype), kind="ExternalInput").ap())
    for i, (shape, dtype) in enumerate(_OUTS):
        dt = _mybir.dt.from_np(_np.dtype(dtype))
        args.append(nc.dram_tensor(f"out_{i}_dram", shape, dt, kind="ExternalOutput").ap())
    build(nc, *args)
    r = _run(nc, [arrays], core_ids=[0])
    got = tuple(r.results[0][f"out_{i}_dram"] for i in range(len(_OUTS)))
    return got[0]
```

```python
import math
from contextlib import ExitStack

import numpy as np
import concourse.bass as bass
from concourse import mybir

F32 = mybir.dt.float32
F32R = mybir.dt.float32r
ALU = mybir.AluOpType
ACT = mybir.ActivationFunctionType
AX = mybir.AxisListType.X

P = 128
D = 1024
KD = D // P
L = 256
T = 2 * L
NT = T // P
DEPTH = 2
BR_W = 512
HEADS = 4
DFF = 4 * D
N_BRANCH = 4
OFF_AQ, OFF_AK, OFF_AV, OFF_HY, OFF_FN, OFF_DN, OFF_DZ, OFF_DA = 0, 512, 1024, 1536, 3072, 3584, 5120, 5632
EPS = 1e-6
GRID_W = 64
HY_EMB, HY_HID = 33, 64
STRIP = 256
KS = 4
RAW = 4
RING = 2
UNITS = 4
WORK = 4
MODS = 48
ATT, HY, FN, DN = range(N_BRANCH)

TABLE = {}


def constant_table():
    parts = []
    tables = []

    def end_table():
        tables.append(np.ascontiguousarray(np.concatenate(parts, 1).astype(np.float32)))
        parts.clear()

    def put(name, a):
        a = np.asarray(a, np.float64)
        full = np.zeros((P, a.shape[1]))
        full[:a.shape[0]] = a
        start = sum(p.shape[1] for p in parts)
        TABLE[name] = (start, a.shape[1])
        parts.append(full)

    i, j = np.arange(P)[:, None], np.arange(P)[None, :]
    put("ident", i == j)
    put("ones", np.ones((P, P)))
    put("tri0", i <= j)
    put("tri1", i >= j)
    put("far0", np.where(j <= i, 0.0, 1e30))
    put("far1", np.where(j >= i, 0.0, 1e30))
    same = lambda n: i // n == j // n
    put("blk0", same(16) & (j < i))
    put("blk1", same(16) & (j > i))
    for n in (32, 64, 128):
        put(f"off{n}", same(n) & ~same(n // 2))
    inv_f = np.float32(10000.0) ** (-np.arange(16, dtype=np.float32) / np.float32(16))
    pos = np.arange(L, dtype=np.float32)
    rope = np.stack([np.floor(pos / GRID_W)[:, None] * inv_f, (pos % GRID_W)[:, None] * inv_f], 1)
    rope = rope.astype(np.float32).astype(np.float64).reshape(2, P, 32).transpose(1, 0, 2).reshape(P, -1)
    put("cos", np.cos(rope))
    put("sin", np.sin(rope))
    put("eps", np.full((P, 1), EPS))
    put("one", np.ones((P, 1)))
    end_table()
    t, f = np.arange(L)[:, None], np.arange(L)[None, :]
    ang = np.pi * ((t * f) % (2 * L)) / L
    fwd = np.concatenate([np.cos(ang), -np.sin(ang)], 1)
    fwd[:, L] = (-1.0) ** np.arange(L)
    put("dft", fwd.reshape(2, P, 2 * L).transpose(1, 0, 2).reshape(P, -1))
    inv = np.concatenate([np.cos(ang).T, -np.sin(ang).T], 0) * 2 / (2 * L)
    inv[0] = 1 / (2 * L)
    inv[L] = (-1.0) ** np.arange(L) / (2 * L)
    put("idft", inv.reshape(4, P, L).transpose(1, 0, 2).reshape(P, -1))
    end_table()
    ca = 2 * np.pi * ((i * j) % P) / P
    put("fn_ch", np.concatenate([np.cos(ca), np.sin(ca)], 1) / math.sqrt(P))
    t, f = np.arange(L)[:, None], np.arange(L)[None, :]
    la = 2 * np.pi * ((t * f) % L) / L
    put("fn_tok", (np.concatenate([np.cos(la), -np.sin(la)], 1) / math.sqrt(L)).reshape(2, P, 2 * L)
        .transpose(1, 0, 2).reshape(P, -1))
    end_table()
    tt = np.linspace(0.0, 1.0, L, dtype=np.float32)[:, None].astype(np.float64)
    w = 2.0 * math.pi * np.arange(L)[:, None] / L
    bands = np.linspace(1e-4, 15, 16)[None]
    put("feats", np.concatenate([tt, np.cos(bands * w), -np.sin(bands * w)], 1).T)
    end_table()
    deltas = np.abs(np.linspace(math.log(1e-2) / 1.5, math.log(1e-2) / 0.3, BR_W))
    dec = np.exp(-tt * deltas)
    back = dec.copy()
    back[0] = 0.0
    decay = np.stack([dec.reshape(2, P, BR_W), back.reshape(2, P, BR_W)], 2).transpose(1, 0, 2, 3)
    return tables + [np.ascontiguousarray(decay.reshape(P, -1)).astype(np.float32)]


def build(nc, x, c, ctx, c_ctx, w_ada, b_ada, norm1, norm2, w_in, attn_qk_gain, attn_lambda, attn_subln,
          hy_conv, hy_w1, hy_b1, hy_freq, hy_w2, hy_b2, hy_w3, hy_bias, dn_conv, dn_a_log, dn_dt_bias,
          dn_norm, w_gate, w_branch, w_o, w_mlp1, w_mlp2, table, hy_table, fn_table, feats_table, decay, out):
    es = ExitStack()
    with es:
        def sb(name, shape):
            return es.enter_context(nc.sbuf_tensor(name, shape, F32))

        def sem(name):
            return es.enter_context(nc.semaphore(name))

        tab = sb("tab", [P, table.shape[1]])
        xT = sb("xT", [P, KD, T])
        raw = sb("raw", [P, RAW, KS, STRIP])
        rows = sb("rows", [P, 2, P])
        cols = sb("cols", [P, DEPTH, 2, P])
        mod = sb("mod", [P, DEPTH, MODS, 2])
        modrow = rows[:].rearrange("p a c -> p (a c)")
        amp = sb("amp", [P, DEPTH, 2, KD, 2])
        rstd = sb("rstd", [P, T])
        tmp = sb("tmp", [P, 2, T])
        wab = sb("wab", [P, KD, 16])
        vecs = sb("vecs", [P, 2 * 64 + P + P + 256 + 8 + 8])
        qkgain = vecs[:, 0:128]
        subln = vecs[:, 128:256]
        dnnorm = vecs[:, 256:384]
        lamv = vecs[:, 384:640]
        alog = vecs[:, 640:648]
        dtb = vecs[:, 648:656]
        small = sb("small", [P, 704])
        csil = sb("csil", [P, KD, 2])

        def sbr(name, shape):
            return es.enter_context(nc.sbuf_tensor(name, shape, F32R))

        whl = sbr("whl", [P, RING, 2, KS, STRIP])
        hhl = sbr("hhl", [P, 2, KD, T])
        chl = sbr("chl", [P, 2, KD, 2])
        wab_hl = sbr("wab_hl", [P, 2, KD, 16])
        BIG = 26624
        with nc.sbuf_tensor("big", [P, BIG], F32) as big:
            pass
        bigr = sbr("bigr", [P, BIG])
        y = big[:, 0:N_BRANCH * HEADS * T].rearrange("p (n h t) -> p n h t", n=N_BRANCH, h=HEADS)
        ARENA0 = N_BRANCH * HEADS * T
        ARENA = BIG - ARENA0
        arena = big[:, ARENA0:BIG]
        arena_r = bigr[:, ARENA0:BIG]

        def carve(*shapes, at=0, arena=arena):
            views = []
            for s in shapes:
                n = int(np.prod(s))
                v = arena[:, at:at + n]
                assert len(s) < 5
                if len(s) == 2:
                    v = v.rearrange("p (a b) -> p a b", a=s[0])
                if len(s) == 3:
                    v = v.rearrange("p (a b c) -> p a b c", a=s[0], b=s[1])
                if len(s) == 4:
                    v = v.rearrange("p (a b c d) -> p a b c d", a=s[0], b=s[1], c=s[2])
                views.append(v)
                at += n
            assert at <= ARENA, at
            return views if len(views) > 1 else views[0]

        def const(name, rows_=P):
            a, n = TABLE[name]
            return tab[0:rows_, a:a + n]

        ident, ones = const("ident"), const("ones")
        eps, one = const("eps"), const("one")

        psum = es.enter_context(nc.psum_tensor("psum", [P, 8, 512], F32))
        unit_bank = [psum[:, b, :] for b in range(UNITS)]
        work_bank = [psum[:, UNITS + b, :] for b in range(WORK)]

        hy_tab = y[:, FN].rearrange("p h t -> p (h t)")
        dft = hy_tab[:, 0:1024].rearrange("p (t f) -> p t f", t=2)
        idft = hy_tab[:, 1024:2048].rearrange("p (k t) -> p k t", k=4)
        ropes = [const(n).rearrange("p (t a f) -> p t a f", t=2, a=2) for n in ("cos", "sin")]

        stage = carve((NT, D))
        SCR = ["dI", "A", "IT", "ITt", "P1", "P2", "U", "P3", "P4", "P5", "Un", "S"]
        qkvT, scr = carve((12, T), (2, len(SCR), BR_W))
        k_tok = y[:, HY].rearrange("p h t -> p (h t)").rearrange("p (m n) -> p m n", m=NT)
        v_tok = y[:, FN].rearrange("p h t -> p (h t)").rearrange("p (m n) -> p m n", m=NT)
        DS = [{n: scr[:, d, i, :] for i, n in enumerate(SCR)} for d in range(2)]
        P2U = [scr[:, d, SCR.index("P2"):SCR.index("U") + 1, :] for d in range(2)]
        dz_tok = qkvT[:, 8:12, :]
        o_dn = y[:, ATT]
        a_qk, a_v, a_qT, a_kT, a_P, a_aT, a_o, a_sq = carve((2, NT, BR_W), (NT, BR_W), (HEADS, T), (HEADS, T),
                                                           (2, 2, T), (HEADS, T), (NT, BR_W), (2, BR_W))
        AT = {"qk": a_qk, "v": a_v, "qT": a_qT, "kT": a_kT, "P": [a_P[:, 0], a_P[:, 1]], "aT": a_aT, "o": a_o}
        HYB = dict(zip(("z0", "z1", "K", "cb", "inv", "zt", "bias", "u"),
                       carve((4, BR_W), (4, BR_W), (2, 5, BR_W), (2, T), (BR_W,), (BR_W,), (2, BR_W), (NT, 3, BR_W))))
        u_at = 4096 + 5120 + 1024 + 1024 + 1024
        HYB |= dict(zip(("w1", "w2", "s", "arg", "turns", "feats", "w3", "decay"),
                        carve((64,), (64,), (L,), (L,), (L,), (L,), (2, 2 * BR_W), (2, 2, BR_W), at=u_at)))
        fn_u_, fn_v_, fn_tab = carve((HEADS, T), (2, HEADS, 2, 2 * P), (5 * L,))
        fch = fn_tab[:, 0:L]
        ftok = fn_tab[:, L:5 * L].rearrange("p (t n) -> p t n", t=2)
        FNB = {"u": fn_u_, "v": fn_v_}
        m_acc, m_sg = carve((KD, T), (4, T))
        y_hl, acc_hl = carve((2, HEADS, T), (2, KD, T), at=6144, arena=arena_r)
        a_hl = carve((2, DFF // P // 2, T), arena=arena_r)
        outs = carve((2, D))

        gv = small[:, 0:32].rearrange("p (t e) -> p t e", t=NT)

        def sm(a, n=32):
            return small[:, a:a + n]

        G_, BETA, GC, EGC, ETOT, EDL, BEG, SC = 0, 32, 64, 160, 192, 224, 256, 288
        O_STAT, QK_STAT, LAM, MAXC, SUMC, HYC = 416, 448, 560, 580, 600, 620
        MT = [[0, 1, 2, 3], [1, 0, 3, 2]]
        COPIES = ["dIT", "A2", "B2", "A4", "A8", "V0", "Y0", "V1", "Y1", "V2", "Y2", "vn"]
        NC_ = len(COPIES)
        ROWS_DONE = [7 * 16, 12 * 16]
        HYW, HYF = 4 * 16, 7 * 16
        TWO_PI = (6.28125, 0.0019340515136718750, 2 * math.pi - 6.28125 - 0.0019340515136718750)
        ROUND = 12582912.0

        def reads_out(li, step):
            return li < DEPTH - 1 or step >= 2

        def o_visits(li):
            return 4 if li == 0 else 6

        def onum(li, br, i):
            n = NT if li == 0 else 2
            return (0 if li == 0 else 2 * NT) + (0 if br == DN else n) + i + 1

        def att_n(li, i, h):
            return 16 * li + 4 * i + h

        def cv(li, key, blk):
            return 24 * li + (0 if key == "dn" else 12) + blk + 1

        def hyz(li, n, s):
            return 2 * n + s if li == 0 else 4 + n

        def fnn(li, s, g):
            return 4 * s + g if li == 0 else 8 + g

        def yt(li):
            return 20 if li == 0 else 30

        consts_loaded = sem("consts_loaded")
        rows_loaded = sem("rows_loaded")
        x_loaded = sem("x_loaded")
        vecs_loaded = sem("vecs_loaded")
        hyw_loaded = sem("hyw_loaded")
        hyf_loaded = sem("hyf_loaded")
        fnw_loaded = sem("fnw_loaded")
        strip_loaded = [sem(f"strip_loaded{i}") for i in range(RAW)]
        unit_done = sem("unit_done")
        unit_free = [sem(f"unit_free{b}") for b in range(UNITS)]
        filled = sem("filled")
        work_free = [sem(f"work_free{b}") for b in range(WORK)]
        act_step, dve_step, pool_step = sem("act_step"), sem("dve_step"), sem("pool_step")
        act_left, dve_left, pool_left = sem("act_left"), sem("dve_left"), sem("pool_left")
        names = ("cols_ready cT_ready sq_ready sum_taken rstd_ready h_ready x_ready x_added gate_cols "
                 "g_ready decays_ready block_conv block_silu block_sq block_rstd block_normed block_tok "
                 "token_copied seg_ready o_normed y_turned stat_ready stat_root q_ready k_ready qkT_ready max_ready "
                 "exp_ready a_ready aT_ready o_copied hyf_arg hyf_sin hyf_taps z_ready zf_ready hy_u fn_u fn_v "
                 "sg_ready mul_done acc_added relu_ready out_ready out_stored hi_ready lo_ready modrow_ready "
                 "clo_ready hn_ready hhi_ready hyf_done yhi_ready ysplit acc_split wab_split").split()
        S = {n: sem(n) for n in names}
        mlp_ready = [sem(f"mlp_ready{i}") for i in range(2)]
        square_step = [sem(f"square_step{i}") for i in range(2)]
        dnames = ("trig_ready far_ready dI_ready A_ready IT_ready blk_ready U_ready aoff_ready copied vb_ready "
                  "kdec_ready r_ready S_ready o_added").split()
        SD = {n: [sem(f"{n}{d}") for d in range(2)] for n in dnames}

        counts = {}

        def link(eng, ins, s):
            k = (str(eng.engine), s.name)
            counts[k] = counts.get(k, 0) + 1
            ins.then_inc(s, 1)
            eng.wait_ge(s, counts[k])

        def signals(eng, ins, s):
            k = (str(eng.engine), s.name)
            counts[k] = counts.get(k, 0) + 1
            ins.then_inc(s, 1)

        strips = []
        strip_end = []
        first_strip, first_unit, first_mark = {}, {}, {}
        at_unit = at_mark = 0

        def add(key, li, sources, marks, units):
            nonlocal at_unit, at_mark
            first_strip[key, li], first_unit[key, li], first_mark[key, li] = len(strips), at_unit, at_mark
            for src, n in zip(sources, marks):
                strips.append(src)
                at_mark += n
                strip_end.append(at_mark)
            at_unit += units

        def by_columns(w, off, n):
            return [w[512 * kh:512 * (kh + 1), off + STRIP * s:off + STRIP * (s + 1)]
                    .rearrange("(k p) n -> p k n", p=P) for s in range(n // STRIP) for kh in range(2)]

        PAIRS = [(0, 1), (1,)]
        MODGROUPS = 6 * D // STRIP

        FIRST_MODS = 2 * D // STRIP

        def add_mods(li, groups):
            for g in groups:
                add(("mod", g), li, by_columns(w_ada[li], STRIP * g, STRIP), [1, 1], 1)
        add_mods(0, range(FIRST_MODS))
        for li in range(DEPTH):
            np_ = len(PAIRS[li])
            add("dn", li, by_columns(w_in[li], OFF_DN, 1536), [1, 2] * 6, 12)
            if li == 0:
                add_mods(1, range(MODGROUPS))
            add("dz", li, by_columns(w_in[li], OFF_DZ, 512), [1, np_] * 2, 2 * np_)
            add("aq", li, by_columns(w_in[li], OFF_AQ, 512), [1, np_] * 2, 2 * np_)
            add("ak", li, by_columns(w_in[li], OFF_AK, 512), [1, 2] * 2, 4)
            add("av", li, by_columns(w_in[li], OFF_AV, 512), [1, 2] * 2, 4)
            if li == 0:
                add_mods(0, range(FIRST_MODS, MODGROUPS))
            add("hy", li, by_columns(w_in[li], OFF_HY, 1536), [1, 2] * 6, 12)
            add("fn", li, by_columns(w_in[li], OFF_FN, 512), [1, 2] * 2, 4)
            add("merge", li, [None] * 48, [1, 2, 1, 2, 2, 2] * 8, 64)
            add("wo", li, by_columns(w_o[li], 0, D), [1, 2] * 4, 8)
            for hf in range(2):
                add(("mlp1", hf), li, [None] * 16, [1, 2] * 8, 16)
                add(("mlp2", hf), li, [None] * 16, [2] * 16, 8)

        def mod_place(li, g):
            if li:
                return FIRST_MODS + g
            return g if g < FIRST_MODS else MODGROUPS + g

        def strip_loop(key, li):
            s0, u0, m0 = first_strip[key, li], first_unit[key, li], first_mark[key, li]
            assert s0 % RAW == 0 and u0 % UNITS == 0
            return s0, u0, m0

        def toks(li):
            return slice(0, T) if li < DEPTH - 1 else slice(L, T)

        def tiles(li):
            return range(NT) if li < DEPTH - 1 else range(2, NT)

        def streams(li):
            return range(2) if li < DEPTH - 1 else range(1, 2)

        block = es.enter_context(nc.Block())
        fill_at = {}

        @block.tensor
        def _(pe):
            n_fill = [0]
            n_unit = [0]
            n_strip = [0]

            def fill(key):
                n = n_fill[0]
                n_fill[0] += 1
                fill_at[key] = n
                if n >= WORK:
                    pe.wait_ge(work_free[n % WORK], n // WORK)
                return work_bank[n % WORK]

            def strip():
                n = n_strip[0]
                n_strip[0] += 1
                pe.wait_ge(S["lo_ready"], n + 1)
                return whl[:, n % RING]

            def unit():
                n = n_unit[0]
                n_unit[0] += 1
                if n >= UNITS:
                    pe.wait_ge(unit_free[n % UNITS], n // UNITS)
                return unit_bank[n % UNITS]

            def mm(o_, a, b, start=True, stop=True):
                return nc.tensor.matmul(o_, a, b, start=start, stop=stop)

            def mm3(o_, a, b, first, last, shared=False):
                for i, (p_, q_) in enumerate(((0, 0), (1, 0), (0, 1))):
                    m = nc.tensor.matmul(o_, a(p_), b(q_), start=first and i == 0, stop=last and i == 2,
                                         skip_group_check=shared)
                return m

            def block_products(bank, w, cb, act, k0, kh, nk, tk):
                for k in range(KS):
                    m = mm3(bank[:, tk], lambda p_: w[:, p_, k, cb * P:(cb + 1) * P],
                            lambda q_: act(q_, k0 + k), kh + k == 0, kh == nk - 1 and k == KS - 1)
                return m

            def feature_strips(key, li, act, tk, after=None):
                assert first_strip[key, li] == n_strip[0] and first_unit[key, li] == n_unit[0]
                n_blocks = {"dn": 12, "hy": 12, "fn": 4, "wo": 8}[key]
                for s_ in range(n_blocks // 2):
                    banks = [unit(), unit()]
                    for kh in range(2):
                        w = strip()
                        for cb in range(2):
                            m = block_products(banks[cb], w, cb, act, KS * kh, kh, 2, tk)
                            if kh or cb:
                                m.then_inc(unit_done, 1)
                            if kh and after:
                                after(2 * s_ + cb)

            def h_part(tk):
                return lambda q_, k: hhl[:, q_, k, tk]

            def token_strips(key, li, pairs):
                assert first_strip[key, li] == n_strip[0] and first_unit[key, li] == n_unit[0]
                for _ in range(2):
                    banks = [unit() for pr in pairs]
                    for kh in range(2):
                        w = strip()
                        for pr, bank in zip(pairs, banks):
                            for mi in range(2):
                                t0 = (2 * pr + mi) * P
                                for k in range(KS):
                                    m = mm3(bank[:, mi * STRIP:(mi + 1) * STRIP],
                                            lambda p_: hhl[:, p_, KS * kh + k, t0:t0 + P],
                                            lambda q_: w[:, q_, k, :], kh + mi + k == 0,
                                            kh == 1 and k == KS - 1, shared=True)
                            if kh == 1 or pr == pairs[-1]:
                                m.then_inc(unit_done, 1)

            def mod_group(li, g):
                assert first_strip[("mod", g), li] == n_strip[0]
                if mod_place(li, g) > FIRST_MODS and (li, g) != (0, FIRST_MODS):
                    mod_turn(li, g - 1)
                bank = unit()
                for kh in range(2):
                    w = strip()
                    for k in range(KS):
                        m = mm3(bank[0:2, 0:STRIP], lambda p_: chl[:, p_, KS * kh + k, :], lambda q_: w[:, q_, k, :],
                                kh + k == 0, kh == 1 and k == KS - 1)
                    m.then_inc(unit_done, 1)
                if 0 < mod_place(li, g) < FIRST_MODS:
                    mod_turn(li, g - 1)

            def mod_turn(li, g):
                pe.wait_ge(S["modrow_ready"], mod_place(li, g) + 1)
                b = fill(("mod", li, g))
                for i in range(2):
                    m = nc.tensor.transpose(b[:, 2 * i:2 * i + 2], modrow[0:2, i * P:(i + 1) * P], ident[0:2, 0:2])
                m.then_inc(filled, 1)

            def turn(bank, src, ids=ident):
                for i, s in enumerate(src):
                    m = nc.tensor.transpose(bank[:, i * P:(i + 1) * P], s, ids)
                return m

            def start_():
                for li in range(DEPTH):
                    pe.wait_ge(rows_loaded, ROWS_DONE[li])
                    if li == 0:
                        pe.wait_ge(consts_loaded, 16)
                    b = fill(("cols", li))
                    nc.tensor.transpose(b[:, 0:100], rows[0:100, 0, :], ident[0:100, 0:100])
                    n = 52 if li == 0 else 36
                    nc.tensor.transpose(b[:, 128:128 + n], rows[0:n, 1, :], ident[0:n, 0:n]).then_inc(filled, 1)
                pe.wait_ge(x_loaded, 32)
                for k in range(KD):
                    b = fill(("x", k))
                    turn(b, [stage[:, m, k * P:(k + 1) * P] for m in range(NT)]).then_inc(filled, 1)
                pe.wait_ge(S["clo_ready"], 1)
                for g in range(FIRST_MODS):
                    mod_group(0, g)
                mod_turn(0, FIRST_MODS - 1)

            def norm(li, which):
                tk = toks(li) if which else slice(0, T)
                n = 2 * li + which
                b = fill(("ms", li, which))
                for k in range(KD):
                    pe.wait_ge(S["sq_ready"], KD * n + k + 1)
                    m = mm(b[:, tk], ones, tmp[:, k % 2, tk], k == 0, k == KD - 1)
                    if k < KD - 1:
                        m.then_inc(S["sum_taken"], 1)
                m.then_inc(filled, 1)

            def dn(li):
                pe.wait_ge(S["h_ready"], 2 * li + 1)
                pe.wait_ge(vecs_loaded, 7 * 16 * (li + 1))
                b = fill(("dab", li))
                pe.wait_ge(S["wab_split"], li + 1)
                for m_ in range(NT):
                    for k in range(KD):
                        m = mm3(b[:, 16 * m_:16 * m_ + 16], lambda p_: hhl[:, p_, k, m_ * P:(m_ + 1) * P],
                                lambda q_: wab_hl[:, q_, k, :], k == 0, k == KD - 1)
                m.then_inc(filled, 1)
                feature_strips("dn", li, h_part(slice(0, T)), slice(0, T))
                pe.wait_ge(S["g_ready"], li + 1)
                b = fill(("gcum", li))
                bt = b[:, 0:32].rearrange("p (t e) -> p t e", t=NT)
                for d in range(2):
                    mm(bt[:, :, 4 * d:4 * d + 4], const(f"tri{d}"), gv[:, :, 4 * d:4 * d + 4])
                m = mm(b[:, 32:64], ones, small[:, 0:32])
                m.then_inc(filled, 1)
                for blk in range(8):
                    pe.wait_ge(S["block_sq"], li * 8 + blk + 1)
                    b = fill(("ss", li, blk))
                    mm(b, ones, tmp[:, blk % 2, :]).then_inc(filled, 1)
                pe.wait_ge(S["block_normed"], li * 8 + 8)
                for blk in range(4, 12):
                    if blk < 8:
                        pe.wait_ge(S["block_normed"], li * 8 + blk + 1)
                    else:
                        pe.wait_ge(S["block_silu"], li * 12 + blk + 1)
                    b = fill(("tok", li, blk))
                    turn(b, [qkvT[:, blk, m_ * P:(m_ + 1) * P] for m_ in range(NT)]).then_inc(filled, 1)
                for step in range(4):
                    q = li * 4 + step
                    sc = [(d, DS[d], MT[d][step]) for d in range(2)]

                    def heads(b, a, r, lvl=None):
                        for h in range(HEADS):
                            m = mm(b[:, h * P:(h + 1) * P], a(h), r(h))
                        m.then_inc(filled, 1)

                    for d, s, m_ in sc:
                        pe.wait_ge(SD["trig_ready"][d], q + 1)
                        b = fill(("gcb", q, d))
                        mm(b, ones, s["P5"]).then_inc(filled, 1)
                    hs = lambda t: (lambda h: t[:, h * P:(h + 1) * P])

                    def weave(i):
                        if li == 0 and i < MODGROUPS:
                            mod_group(1, i)
                    weave(6 * step)
                    for d, s, m_ in sc:
                        pe.wait_ge(SD["dI_ready"][d], q + 1)
                        turn(fill(("dIT", q, d)), [hs(s["dI"])(h) for h in range(4)]).then_inc(filled, 1)
                    for d, s, m_ in sc:
                        for hp in range(2):
                            b = fill((f"kq{hp}", q, d))
                            for i in range(2):
                                h = 2 * hp + i
                                m = mm(b[:, i * STRIP:(i + 1) * STRIP], qkvT[:, 4 + h, m_ * P:(m_ + 1) * P],
                                       qkvT[:, h:h + 5:4, m_ * P:(m_ + 1) * P])
                            m.then_inc(filled, 1)
                    for d, s, m_ in sc:
                        pe.wait_ge(SD["A_ready"][d], q + 1)
                        turn(fill(("B", q, d)), [hs(s["A"])(h) for h in range(4)]).then_inc(filled, 1)

                    def prod(nm, a, r, waits):
                        for d, s, m_ in sc:
                            for wn, wk in waits:
                                pe.wait_ge(SD[wn][d], wk)
                            b = fill((nm, q, d))
                            heads(b, hs(s[a]), hs(s[r]))

                    cp = lambda nm: ("copied", q * NC_ + COPIES.index(nm) + 1)
                    prod("A2", "Un", "dI", [("blk_ready", 3 * q + 2)])
                    prod("B2", "dI", "Un", [])
                    weave(6 * step + 1)
                    prod("A4", "P2", "P1", [cp("B2")])
                    for d, s, m_ in sc:
                        pe.wait_ge(SD["blk_ready"][d], 3 * q + 3)
                        for hp in range(2):
                            b = fill((f"BU{hp}", q, d))
                            for i in range(2):
                                h = 2 * hp + i
                                m = mm(b[:, i * STRIP:(i + 1) * STRIP], hs(s["P1"])(h),
                                       P2U[d][:, :, h * P:(h + 1) * P])
                            m.then_inc(filled, 1)
                    weave(6 * step + 2)
                    prod("A8", "P4", "P3", [("U_ready", 6 * q + 1)])
                    prod("Ub", "P3", "Un", [])
                    weave(6 * step + 3)
                    prod("Uc", "P5", "U", [cp("A8"), ("U_ready", 6 * q + 2)])
                    cur, nxt = "Un", "U"
                    for lv in range(3):
                        for d, s, m_ in sc:
                            pe.wait_ge(SD["U_ready"][d], 6 * q + 3 + lv)
                            turn(fill((f"V{lv}", q, d)), [hs(s[cur])(h) for h in range(4)]).then_inc(filled, 1)
                        prod(f"Y{lv}", "dI", cur, [("aoff_ready", 3 * q + lv + 1)])
                        prod(f"M{lv}", "P2", "P4", [cp(f"V{lv}"), cp(f"Y{lv}")])
                        if lv < 2:
                            weave(6 * step + 4 + lv)
                        cur, nxt = nxt, cur
                    for d, s, m_ in sc:
                        if step == 0:
                            pe.wait_ge(S["seg_ready"], 2 * (li + 1))
                        else:
                            pe.wait_ge(SD["S_ready"][d], q - li)
                        b = fill(("KS", q, d))
                        heads(b, lambda h: qkvT[:, 4 + h, m_ * P:(m_ + 1) * P], hs(s["S"]))
                        if reads_out(li, step):
                            b = fill(("qS", q, d))
                            heads(b, lambda h: qkvT[:, h, m_ * P:(m_ + 1) * P], hs(s["S"]))
                    prod("vn", "U", "P1", [("r_ready", q + 1), ("U_ready", 6 * q + 6)])
                    if reads_out(li, step):
                        prod("iv", "ITt", "P3", [cp("vn"), ("IT_ready", q + 1)])
                    if step < 3:
                        prod("kv", "IT", "P3", [cp("vn"), ("kdec_ready", q + 1)])
                if li == 0:
                    mod_turn(1, MODGROUPS - 1)
                token_strips("dz", li, (0, 1) if li < DEPTH - 1 else (1,))
                for i, m_ in enumerate(tiles(li)):
                    pe.wait_ge(S["o_normed"], onum(li, DN, i))
                    b = fill(("yd", li, m_))
                    turn(b, [y[:, ATT, m_, h * P:(h + 1) * P] for h in range(4)]).then_inc(filled, 1)

            def att(li):
                token_strips("aq", li, (0, 1) if li < DEPTH - 1 else (1,))
                token_strips("ak", li, (0, 1))
                token_strips("av", li, (0, 1))
                A = AT
                for which in range(2):
                    tl = tiles(li) if which == 0 else range(NT)
                    for h in range(HEADS):
                        pe.wait_ge(S["k_ready" if which else "q_ready"], li + 1)
                        b = fill(("qkT", li, which, h))
                        for m_ in tl:
                            m = nc.tensor.transpose(b[:, m_ * P:(m_ + 1) * P],
                                                    A["qk"][:, which, m_, h * P:(h + 1) * P], ident)
                        m.then_inc(filled, 1)
                for i, m_ in enumerate(tiles(li)):
                    nk = 2 if m_ < 2 else 4

                    def turned(h):
                        n = att_n(li, i, h)
                        pe.wait_ge(S["a_ready"], n + 1)
                        b = fill(("aT", li, m_, h))
                        turn(b, [A["P"][h % 2][:, 0, kt * P:(kt + 1) * P] for kt in range(nk)]).then_inc(filled, 1)
                    for h in range(HEADS):
                        if i == 0 and h == 0:
                            pe.wait_ge(S["qkT_ready"], 8 * (li + 1))
                        for cc in range(2):
                            b = fill(("s", li, m_, h, cc))
                            sl = slice(64 * cc, 64 * cc + 64)
                            mm(b[:, 0:nk * P], A["qT"][sl, h, m_ * P:(m_ + 1) * P],
                               A["kT"][sl, h, 0:nk * P]).then_inc(filled, 1)
                        if li == 0:
                            mod_group(0, FIRST_MODS + HEADS * i + h)
                        if h > 0:
                            turned(h - 1)
                    turned(HEADS - 1)
                    b = fill(("o", li, m_))
                    pe.wait_ge(S["aT_ready"], att_n(li, i, 3) + 1)
                    for h in range(HEADS):
                        for kt in range(nk):
                            m = mm(b[:, h * P:(h + 1) * P], A["aT"][:, h, kt * P:(kt + 1) * P],
                                   A["v"][:, kt, h * P:(h + 1) * P], kt == 0, kt == nk - 1)
                    m.then_inc(filled, 1)
                if li == 0:
                    assert FIRST_MODS + HEADS * NT == MODGROUPS
                    mod_turn(0, MODGROUPS - 1)
                for i, m_ in enumerate(tiles(li)):
                    pe.wait_ge(S["o_normed"], onum(li, ATT, i))
                    b = fill(("ya", li, m_))
                    turn(b, [A["o"][:, m_, h * P:(h + 1) * P] for h in range(4)]).then_inc(filled, 1)

            def hyena(li):
                H_ = HYB
                pe.wait_ge(hyf_loaded, HYF * (li + 1))
                b = fill(("f1", li))
                mm(b[0:HY_HID, 0:L], H_["w1"][0:HY_EMB, :], H_["feats"][0:HY_EMB, :]).then_inc(filled, 1)
                pe.wait_ge(S["hyf_sin"], 2 * li + 1)
                b = fill(("f2", li))
                mm(b[0:HY_HID, 0:L], H_["w2"][0:HY_HID, :], H_["s"][0:HY_HID, :]).then_inc(filled, 1)
                pe.wait_ge(S["hyf_sin"], 2 * li + 2)
                pe.wait_ge(hyw_loaded, HYW * (li + 1))
                for n in range(2):
                    for tt in range(2):
                        for dr in range(2):
                            b = fill(("f3", li, n, tt, dr))
                            mm(b, H_["s"][0:HY_HID, tt * P:(tt + 1) * P],
                               H_["w3"][0:HY_HID, n, dr * 512:(dr + 1) * 512]).then_inc(filled, 1)
                    pe.wait_ge(S["hyf_taps"], 2 * li + n + 1)
                    b = fill(("fs", li, n))
                    for tt in range(2):
                        for dr in range(2):
                            m = mm(b, ones, H_["z1"][:, 2 * tt + dr, :], tt + dr == 0, tt + dr == 2)
                    m.then_inc(filled, 1)
                    for fc in range(4):
                        b = fill(("fk", li, n, fc))
                        for tt in range(2):
                            m = mm(b, dft[:, tt, fc * P:(fc + 1) * P], H_["z0"][:, 2 * tt + fc // 2, :],
                                   tt == 0, tt == 1)
                        m.then_inc(filled, 1)
                    b = fill(("fL", li, n))
                    for tt in range(2):
                        m = mm(b, dft[:, tt, 2 * P:3 * P], H_["z0"][:, 2 * tt, :], tt == 0, tt == 1)
                    m.then_inc(filled, 1)
                assert first_strip["hy", li] == n_strip[0]
                tk = toks(li)

                def turned(blk):
                    pe.wait_ge(S["block_conv"], cv(li, "hy", blk))
                    b = fill(("hyu", li, blk))
                    for m_ in tiles(li):
                        m = nc.tensor.transpose(b[:, m_ * P:(m_ + 1) * P], H_["cb"][:, blk % 2, m_ * P:(m_ + 1) * P], ident)
                    m.then_inc(filled, 1)
                feature_strips("hy", li, h_part(tk), tk, after=lambda blk: turned(blk - 2) if blk >= 2 else None)
                turned(10)
                turned(11)
                pe.wait_ge(S["hy_u"], 12 * (li + 1))
                for n in range(2):
                    for s in streams(li):
                        zz = hyz(li, n, s)
                        if n:
                            pe.wait_ge(S["z_ready"], hyz(li, 0, s) + 1)
                        for fc in (0, 2, 1, 3):
                            b = fill(("zf", zz, fc))
                            for tt in range(2):
                                m = mm(b, dft[:, tt, fc * P:(fc + 1) * P], H_["u"][:, 2 * s + tt, 2, :],
                                       tt == 0, tt == 1)
                            m.then_inc(filled, 1)
                        pe.wait_ge(S["zf_ready"], 2 * (zz + 1))
                        for tt in range(2):
                            b = fill(("zt", zz, tt))
                            for i_, fc in enumerate((0, 2, 1, 3)):
                                m = mm(b, idft[:, fc, tt * P:(tt + 1) * P], H_["z0"][:, fc, :], i_ == 0, i_ == 3)
                            m.then_inc(filled, 1)
                for i, m_ in enumerate(tiles(li)):
                    pe.wait_ge(S["z_ready"], hyz(li, 1, m_ // 2) + 1)
                    b = fill(("yh", li, m_))
                    turn(b, [H_["u"][:, m_, 2, h * P:(h + 1) * P] for h in range(4)]).then_inc(filled, 1)

            def fnet(li):
                tk = toks(li)
                feature_strips("fn", li, h_part(tk), tk)
                fn = FNB
                pe.wait_ge(fnw_loaded, 16 * (li + 1))
                pe.wait_ge(S["fn_u"], 4 * (li + 1))
                i = 0
                for s in streams(li):
                    for g in range(HEADS):
                        b = fill(("fv", li, s, g))
                        for tt in range(2):
                            m = mm(b[:, tt * 256:(tt + 1) * 256], fn["u"][:, g, s * L + tt * P:s * L + (tt + 1) * P], fch)
                        m.then_inc(filled, 1)
                for s in streams(li):
                    for g in range(HEADS):
                        pe.wait_ge(S["fn_v"], fnn(li, s, g) + 1)
                        b = fill(("fy", li, s, g))
                        for i_, (tt, w) in enumerate(((0, 0), (0, 1), (1, 0), (1, 1))):
                            m = mm(b[:, 0:L], fn["v"][:, s, g, tt, w * P:(w + 1) * P],
                                   ftok[:, tt, w * L:(w + 1) * L], i_ == 0, i_ == 3)
                        m.then_inc(filled, 1)

            def merge(li):
                tk = toks(li)
                s0, u0, m0 = strip_loop("merge", li)
                assert s0 == n_strip[0] and u0 == n_unit[0]
                n_strip[0] += 48
                n_unit[0] += 64
                with pe.Fori(0, N_BRANCH) as n:
                    for i in range(12):
                        jj, j = i // 6, i % 6
                        w = whl[:, i % RING]
                        pe.wait_ge(S["lo_ready"], s0 + i + 1 + n * 12)
                        if j < 4:
                            for cb in range(2):
                                g = j // 2 * 2 + cb
                                if j % 2 == 0:
                                    pe.wait_ge(unit_free[g], (u0 + 8 * jj) // UNITS + n * 4)
                                m = block_products(unit_bank[g], w, cb, h_part(tk), KS * (j % 2), j % 2, 2, tk)
                                if j % 2 or cb:
                                    m.then_inc(unit_done, 1)
                        else:
                            if i == 4:
                                pe.wait_ge(S["ysplit"], N_BRANCH * li + 1 + n)
                            for cb in range(2):
                                g = 2 * (j - 4) + cb
                                pe.wait_ge(unit_free[g], (u0 + 8 * jj) // UNITS + 1 + n * 4)
                                block_products(unit_bank[g], w, cb, lambda q_, k: y_hl[:, q_, k, tk], 0, 0, 1, tk)\
                                    .then_inc(unit_done, 1)

            def tail(li):
                tk = toks(li)
                pe.wait_ge(S["acc_split"], li + 1)
                feature_strips("wo", li, lambda q_, k: acc_hl[:, q_, k, tk], tk)
                norm(li, 1)
                pe.wait_ge(S["h_ready"], 2 * li + 2)
                for hf in range(2):
                    s0, u0, m0 = strip_loop(("mlp1", hf), li)
                    assert s0 == n_strip[0] and u0 == n_unit[0]
                    n_strip[0] += 16
                    n_unit[0] += 16
                    with pe.Fori(0, 4) as i:
                        for e in range(2):
                            for cb in range(2):
                                pe.wait_ge(unit_free[2 * e + cb], u0 // UNITS + i)
                            for kh in range(2):
                                pe.wait_ge(S["lo_ready"], s0 + 2 * e + kh + 1 + i * 4)
                                for cb in range(2):
                                    m = block_products(unit_bank[2 * e + cb], whl[:, kh], cb, h_part(tk), KS * kh,
                                                       kh, 2, tk)
                                    if kh or cb:
                                        m.then_inc(unit_done, 1)
                    s0, u0, m0 = strip_loop(("mlp2", hf), li)
                    assert s0 == n_strip[0] and u0 == n_unit[0]
                    n_strip[0] += 16
                    n_unit[0] += 8
                    for cb in range(2):
                        pe.wait_ge(mlp_ready[cb], 1 + 8 * (2 * li + hf + 1))
                    with pe.Fori(0, 2) as i:
                        for e in range(2):
                            for cb in range(2):
                                pe.wait_ge(unit_free[2 * e + cb], u0 // UNITS + i)
                            for kc in range(4):
                                pe.wait_ge(S["lo_ready"], s0 + 4 * e + kc + 1 + i * 8)
                                for cb in range(2):
                                    block_products(unit_bank[2 * e + cb], whl[:, kc % RING], cb,
                                                   lambda q_, k: a_hl[:, q_, k, tk], KS * kc, kc, 4, tk)\
                                        .then_inc(unit_done, 1)

            def leave():
                for i in range(4):
                    b = fill(("out", i))
                    pe.wait_ge(S["x_added"], 24 * DEPTH)
                    m_, half = 2 + i // 2, i % 2
                    turn(b, [xT[:, 4 * half + k, m_ * P:(m_ + 1) * P] for k in range(4)]).then_inc(filled, 1)

            start_()
            for li in range(DEPTH):
                norm(li, 0)
                dn(li)
                att(li)
                hyena(li)
                fnet(li)
                merge(li)
                tail(li)
            leave()

        def filled_bank(eng, key):
            n = fill_at[key]
            eng.wait_ge(filled, n + 1)
            return work_bank[n % WORK]

        def give_fill(eng, key):
            eng.sem_inc(work_free[fill_at[key] % WORK], 1)

        def unit_mark(key, li, i):
            per = {"dz": len(PAIRS[li]), "aq": len(PAIRS[li])}.get(key, 2)
            return first_mark[key, li] + (1 + per) * (i // per) + 2 + i % per

        def unit_bank_of(eng, key, li, i):
            eng.wait_ge(unit_done, unit_mark(key, li, i))
            return unit_bank[(first_unit[key, li] + i) % UNITS]

        def split_hi(act, n, i=0, step=0, done=None):
            r = n % RING
            act.wait_ge(strip_loaded[n % RAW], 16 * (n // RAW + 1) + i * (16 * step // RAW))
            if done is not None:
                act.wait_ge(unit_done, done)
            for h in range(2):
                ks = slice(KS // 2 * h, KS // 2 * (h + 1))
                nc.scalar.copy(whl[:, r, 0, ks], raw[:, n % RAW, ks]).then_inc(S["hi_ready"], 1)

        def split_lo(eng, n, i=0, step=0):
            r = n % RING
            for h in range(2):
                ks = slice(KS // 2 * h, KS // 2 * (h + 1))
                eng.wait_ge(S["hi_ready"], 2 * n + h + 1 + i * (2 * step))
                ins = eng.tensor_tensor(whl[:, r, 1, ks], raw[:, n % RAW, ks], whl[:, r, 0, ks].bitcast(F32),
                                        ALU.subtract)
                if h:
                    ins.then_inc(S["lo_ready"], 1)

        def hi_ahead(act, n):
            if n + RING < len(strips):
                split_hi(act, n + RING, done=strip_end[n])

        def lo_ahead(eng, n):
            if n + RING < len(strips):
                split_lo(eng, n + RING)

        def take_over(eng, key, li):
            eng.wait_ge(S["lo_ready"], first_strip[key, li] + RING)

        def give_unit(eng, key, li, i):
            eng.sem_inc(unit_free[(first_unit[key, li] + i) % UNITS], 1)

        left = {"act": act_left, "dve": dve_left, "pool": pool_left}

        def enter(eng, n):
            if n:
                for s_ in left.values():
                    eng.wait_ge(s_, n)

        PHASES = 5

        def ph(li, i):
            return PHASES * li + i

        def bc_heads(v):
            return v.unsqueeze(2).to_broadcast([P, HEADS, P])

        def over_heads(v):
            return v.unsqueeze(1).to_broadcast([P, HEADS, P])

        def hd(v):
            return v.rearrange("p (h n) -> p h n", h=HEADS)

        def square(eng, cb, li, hf, e, i):
            tk, g = toks(li), 2 * e + cb
            n = 8 * (2 * li + hf) + e
            t_ = tmp[:, cb, tk]
            hi, lo = (a_hl[:, o_, bass.ds(i * 4 + g, 1), tk].rearrange("p a t -> p (a t)") for o_ in range(2))
            eng.wait_ge(S["relu_ready"], 16 * (2 * li + hf) + g + 1 + i * 4)
            eng.tensor_tensor(t_, t_, t_, ALU.mult).then_inc(square_step[cb], 1)
            eng.wait_ge(square_step[cb], 2 * n + 1 + i * 4)
            eng.tensor_copy(hi, t_).then_inc(square_step[cb], 1)
            eng.wait_ge(square_step[cb], 2 * n + 2 + i * 4)
            eng.tensor_tensor(lo, t_, hi.bitcast(F32), ALU.subtract).then_inc(mlp_ready[cb], 1)

        def scale_and_turn(eng, step, which, tl, scratch, ready):
            for m_ in tl:
                v = a_qk[:, which, m_, :].rearrange("p (g n) -> p g n", g=8)
                c0 = QK_STAT + 8 * (4 * which + m_)
                last = m_ == NT - 1
                step(eng.tensor_tensor(v, v, small[:, c0:c0 + 8].unsqueeze(2).to_broadcast([P, 8, 64]), ALU.mult))
                step(eng.tensor_tensor(v, v, qkgain[:, 64 * which:64 * which + 64].unsqueeze(1)
                                       .to_broadcast([P, 8, 64]), ALU.mult))
                if m_ >= 2:
                    x5 = a_qk[:, which, m_, :].rearrange("p (g a h f) -> p g a h f", g=8, a=2, h=2)
                    xa, xb = x5[:, :, :, 0, :], x5[:, :, :, 1, :]
                    cs, sn = (r[:, m_ - 2].unsqueeze(1).to_broadcast([P, 8, 2, 16]) for r in ropes)
                    q4 = [scratch[:, i // 2, (i % 2) * 256:(i % 2 + 1) * 256]
                          .rearrange("p (g a f) -> p g a f", g=8, a=2) for i in range(4)]
                    for dst, a, b in ((q4[0], xa, cs), (q4[1], xb, sn), (q4[2], xb, cs), (q4[3], xa, sn)):
                        ins = eng.tensor_tensor(dst, a, b, ALU.mult)
                    step(ins)
                    eng.tensor_tensor(xa, q4[0], q4[1], ALU.subtract)
                    ins = eng.tensor_tensor(xb, q4[2], q4[3], ALU.add)
                    if last:
                        step(ins, ready)
                    else:
                        step(ins)

        @block.sync
        def _(sp):
            def load_rows(li):
                if li:
                    sp.wait_ge(filled, fill_at["cols", 0] + 1)
                for dst, src in ((rows[0:48, 0, :], b_ada[li]), (rows[48:56, 0, :], norm1[li]),
                                 (rows[56:64, 0, :], norm2[li]),
                                 (rows[64:100, 0, :], hy_conv[li].rearrange("a c -> (a c)")),
                                 (rows[0:36, 1, :], dn_conv[li].rearrange("a c -> (a c)"))):
                    sp.dma_start(dst, src.rearrange("(r c) -> r c", c=P)).then_inc(rows_loaded, 16)
                if li == 0:
                    sp.dma_start(rows[36:44, 1, :], c_ctx.rearrange("(r c) -> r c", c=P)).then_inc(rows_loaded, 16)
                    sp.dma_start(rows[44:52, 1, :], c.rearrange("a (r c) -> (a r) c", c=P)).then_inc(rows_loaded, 16)

            def load_strip(n):
                if n >= RAW:
                    sp.wait_ge(S["lo_ready"], n - RAW + 1)
                sp.dma_start(raw[:, n % RAW], strips[n]).then_inc(strip_loaded[n % RAW], 16)

            def load_in_loop(n, i, step, src):
                sp.wait_ge(S["lo_ready"], n - RAW + 1 + i * step)
                sp.dma_start(raw[:, n % RAW], src).then_inc(strip_loaded[n % RAW], 16)

            def load_vecs(li):
                enter(sp, ph(li, 0))
                for dst, src in ((qkgain, attn_qk_gain[li].rearrange("a b -> (a b)")), (subln, attn_subln[li]),
                                 (dnnorm, dn_norm[li]), (lamv, attn_lambda[li].rearrange("a b -> (a b)")),
                                 (alog, dn_a_log[li].rearrange("a b -> (a b)")),
                                 (dtb, dn_dt_bias[li].rearrange("a b -> (a b)"))):
                    sp.dma_start(dst, src.unsqueeze(0).to_broadcast([P, src.shape[0]])).then_inc(vecs_loaded, 16)
                sp.dma_start(wab[:], w_in[li, :, OFF_DA:OFF_DA + 16].rearrange("(k p) n -> p k n", p=P))\
                  .then_inc(vecs_loaded, 16)

            load_rows(0)
            sp.dma_start(tab[:], table).then_inc(consts_loaded, 16)
            sp.dma_start(stage[:, 0:2, :], ctx[0].rearrange("(m p) d -> p m d", p=P)).then_inc(x_loaded, 16)
            sp.dma_start(stage[:, 2:4, :], x[0].rearrange("(m p) d -> p m d", p=P)).then_inc(x_loaded, 16)
            for n in range(first_strip["dn", 0]):
                load_strip(n)
                if n == 1:
                    load_rows(1)
                if n == 7:
                    load_vecs(0)
            for li in range(DEPTH):
                for n in range(first_strip["dn", li], first_strip["merge", li]):
                    if li and n == first_strip["dn", li] + RAW:
                        load_vecs(li)
                    load_strip(n)
                s0, u0, m0 = strip_loop("merge", li)
                with sp.Fori(0, N_BRANCH) as n:
                    for i in range(12):
                        jj, j = i // 6, i % 6
                        if j < 4:
                            kh, a = j % 2, jj * 512 + (j // 2) * STRIP
                            src = w_gate[li, bass.ds(n, 1), 512 * kh:512 * (kh + 1), a:a + STRIP]
                        else:
                            a = jj * 512 + (j - 4) * STRIP
                            src = w_branch[li, bass.ds(n, 1), :, a:a + STRIP]
                        load_in_loop(s0 + i, n, 12, src.rearrange("a (k p) n -> p (a k) n", p=P))
                for n in range(first_strip["wo", li], first_strip[("mlp1", 0), li]):
                    load_strip(n)
                for hf in range(2):
                    s0, u0, m0 = strip_loop(("mlp1", hf), li)
                    with sp.Fori(0, 4) as i:
                        for e in range(2):
                            for kh in range(2):
                                a = bass.ds(i * 2 * STRIP + e * STRIP + hf * DFF // 2, STRIP)
                                src = w_mlp1[li, 512 * kh:512 * (kh + 1), a]
                                load_in_loop(s0 + 2 * e + kh, i, 4, src.rearrange("(k p) n -> p k n", p=P))
                    s0, u0, m0 = strip_loop(("mlp2", hf), li)
                    with sp.Fori(0, 4) as i:
                        for kc in range(4):
                            r0 = hf * DFF // 2 + 512 * kc
                            src = w_mlp2[li, r0:r0 + 512, bass.ds(i * STRIP, STRIP)]
                            load_in_loop(s0 + kc, i, 4, src.rearrange("(k p) n -> p k n", p=P))
            sp.wait_ge(S["out_ready"], 4)
            sp.dma_start(out[0].rearrange("(m p) d -> p m d", p=P), outs).then_inc(S["out_stored"], 16)
            sp.wait_ge(S["out_stored"], 16)

        @block.scalar
        def _(act):
            def step(ins, s_=act_step):
                link(act, ins, s_)

            def f(o_, i_, fn, **kw):
                return nc.scalar.activation(o_, i_, fn, **kw)

            def copy(o_, i_):
                return nc.scalar.copy(o_, i_)

            def rsqrt(o_, i_, n, s_, done=None, after=None):
                step(f(o_, i_, ACT.Ln, bias=eps[0:o_.shape[0]], scale=1.0 / n))
                if after:
                    after()
                step(f(o_, o_, ACT.Exp, scale=-0.5), s_)

            def start_():
                split_hi(act, 0)
                split_hi(act, 1)
                act.wait_ge(S["cols_ready"], 1)
                for s_ in range(2):
                    step(f(csil[:, :, s_], cols[:, 0, 1, 36 + 8 * s_:44 + 8 * s_], ACT.Silu))
                    step(copy(chl[:, 0, :, s_], csil[:, :, s_]), S["cT_ready"])
                for k in range(KD):
                    b = filled_bank(act, ("x", k))
                    step(copy(xT[:, k, :], b), S["x_ready"])
                    give_fill(act, ("x", k))
                for g in range(FIRST_MODS):
                    mod_row(0, g)

            def mod_row(li, g):
                n = first_strip[("mod", g), li]
                hi_ahead(act, n)
                hi_ahead(act, n + 1)
                act.wait_ge(unit_done, strip_end[n + 1])
                if g:
                    act.wait_ge(filled, fill_at["mod", li, g - 1] + 1)
                u = first_unit[("mod", g), li]
                step(copy(modrow[0:2, :], unit_bank[u % UNITS][0:2, 0:STRIP]), S["modrow_ready"])
                act.sem_inc(unit_free[u % UNITS], 1)

            def norm(li, which):
                tk = toks(li) if which else slice(0, T)
                n = 2 * li + which
                if li or which:
                    act.wait_ge(S["x_added"], 24 * li + 8 * which)
                for k in range(KD):
                    if k >= 2:
                        act.wait_ge(S["sum_taken"], (KD - 1) * n + k - 1)
                    f(tmp[:, k % 2, tk], xT[:, k, tk], ACT.Square).then_inc(S["sq_ready"], 1)
                b = filled_bank(act, ("ms", li, which))
                rsqrt(rstd[:, tk], b[:, tk], D, S["rstd_ready"], after=lambda: give_fill(act, ("ms", li, which)))
                for k in range(KD):
                    act.wait_ge(S["hn_ready"], KD * n + k + 1)
                    for s_ in (range(2) if which == 0 else streams(li)):
                        sl = slice(s_ * L, (s_ + 1) * L)
                        ins = f(hhl[:, 0, k, sl], tmp[:, k % 2, sl], ACT.Identity,
                                bias=mod[:, li, 24 * which + k, s_:s_ + 1])
                    ins.then_inc(S["hhi_ready"], 1)

            def dn(li):
                act.wait_ge(S["gate_cols"], 2 * li + 1)
                step(f(sm(SC + 32), sm(SC + 32), ACT.Exp))
                step(f(sm(SC + 32), sm(SC + 32), ACT.Ln, bias=one))
                step(f(sm(SC + 96), sm(SC + 96), ACT.Exp, scale=-1.0))
                step(f(sm(HYC, 8), alog, ACT.Exp), S["decays_ready"])
                def silu(blk):
                    act.wait_ge(S["block_conv"], cv(li, "dn", blk))
                    step(f(qkvT[:, blk, :], qkvT[:, blk, :], ACT.Silu), S["block_silu"])
                n0 = first_strip["dn", li]
                for s_ in range(6):
                    hi_ahead(act, n0 + 2 * s_)
                    hi_ahead(act, n0 + 2 * s_ + 1)
                    if s_:
                        silu(2 * s_ - 2)
                        silu(2 * s_ - 1)
                silu(10)
                silu(11)

                def square(blk):
                    step(f(tmp[:, blk % 2, :], qkvT[:, blk, :], ACT.Square), S["block_sq"])
                square(0)
                square(1)
                for blk in range(8):
                    b = filled_bank(act, ("ss", li, blk))
                    rsqrt(tmp[:, blk % 2, :], b, 1, S["block_rstd"], after=lambda: give_fill(act, ("ss", li, blk)))
                    if blk < 6:
                        act.wait_ge(S["block_normed"], 8 * li + blk + 1)
                        square(blk + 2)
                for blk in range(4, 12):
                    b = filled_bank(act, ("tok", li, blk))
                    dst = k_tok if blk < 8 else v_tok
                    step(copy(dst[:, :, (blk % 4) * P:(blk % 4 + 1) * P], hd(b)), S["block_tok"])
                    give_fill(act, ("tok", li, blk))
                act.wait_ge(S["gate_cols"], 2 * li + 2)
                step(f(sm(EGC, 96), sm(GC, 96), ACT.Exp), S["decays_ready"])
                for st in range(4):
                    q = 4 * li + st

                    def cp(nm, dst):
                        for d in range(2):
                            b = filled_bank(act, (nm, q, d))
                            step(copy(DS[d][dst], b), SD["copied"][d])
                            give_fill(act, (nm, q, d))
                    for d in range(2):
                        act.wait_ge(SD["far_ready"][d], q + 1)
                        for h in range(HEADS):
                            v = DS[d]["dI"][:, h * P:(h + 1) * P]
                            col = GC + 8 * MT[d][st] + 4 * d + h
                            ins = f(v, v, ACT.Exp, bias=small[:, col:col + 1], scale=-1.0)
                        step(ins, SD["dI_ready"][d])

                    def weave(i):
                        if li == 0:
                            mod_row(1, i)
                    weave(6 * st)
                    cp("dIT", "ITt")
                    cp("A2", "P1")
                    cp("B2", "P2")
                    weave(6 * st + 1)
                    cp("A4", "P3")
                    weave(6 * st + 2)
                    cp("A8", "P5")
                    weave(6 * st + 3)
                    for lv in range(3):
                        cp(f"V{lv}", "P2")
                        cp(f"Y{lv}", "P4")
                        if lv < 2:
                            weave(6 * st + 4 + lv)
                    cp("vn", "P3")
                for d in range(2):
                    act.wait_ge(SD["o_added"][d], o_visits(li))
                token_units("dz", li, dz_tok, ACT.Silu)
                stat_root(li, 0, sm(O_STAT, 16), P)
                turned(li, "yd", DN)
                step(copy(small[:, 700:701], one), act_left)

            def token_units(key, li, dst, fn):
                n, u = first_strip[key, li], 0
                prs = PAIRS[li] if key in ("dz", "aq") else (0, 1)
                for s_ in range(2):
                    hi_ahead(act, n + 2 * s_)
                    hi_ahead(act, n + 2 * s_ + 1)
                    for pr in prs:
                        b = unit_bank_of(act, key, li, u)
                        step(f(dst[:, 2 * pr:2 * pr + 2, s_ * STRIP:(s_ + 1) * STRIP],
                               b.rearrange("p (m n) -> p m n", m=2), fn), S["token_copied"])
                        give_unit(act, key, li, u)
                        u += 1

            def stat_root(li, i, v, n):
                act.wait_ge(S["stat_ready"], 3 * li + i + 1)
                rsqrt(v, v, n, S["stat_root"])

            def turned(li, nm, br):
                for m_ in tiles(li):
                    b = filled_bank(act, (nm, li, m_))
                    step(copy(y[:, br, :, m_ * P:(m_ + 1) * P], hd(b)), S["y_turned"])
                    give_fill(act, (nm, li, m_))

            def att(li):
                enter(act, ph(li, 1))
                act.dma_start(hy_tab, hy_table).then_inc(hyw_loaded, 16)
                for key, dst in (("aq", a_qk[:, 0]), ("ak", a_qk[:, 1]), ("av", a_v)):
                    token_units(key, li, dst, ACT.Copy)
                act.wait_ge(S["stat_ready"], 3 * li + 2)
                step(f(sm(LAM, 2), sm(LAM, 2), ACT.Exp))
                stat_root(li, 1, sm(QK_STAT, 64), 64)
                for which, dst in ((0, a_qT), (1, a_kT)):
                    tk = toks(li) if which == 0 else slice(0, T)
                    for h in range(HEADS):
                        b = filled_bank(act, ("qkT", li, which, h))
                        step(copy(dst[:, h, tk], b[:, tk]), S["qkT_ready"])
                        give_fill(act, ("qkT", li, which, h))
                for i, m_ in enumerate(tiles(li)):
                    nk = 2 if m_ < 2 else 4

                    def probs_turned(h):
                        b = filled_bank(act, ("aT", li, m_, h))
                        step(copy(a_aT[:, h, 0:nk * P], b[:, 0:nk * P]), S["aT_ready"])
                        give_fill(act, ("aT", li, m_, h))
                    for h in range(HEADS):
                        n = att_n(li, i, h)
                        for cc in range(2):
                            act.wait_ge(S["max_ready"], 2 * n + cc + 1)
                            b = filled_bank(act, ("s", li, m_, h, cc))
                            par = 2 * (n % 2) + cc
                            step(f(a_P[:, h % 2, cc, 0:nk * P], b[:, 0:nk * P], ACT.Exp, scale=0.125,
                                   bias=small[:, MAXC + 8 + par:MAXC + 9 + par],
                                   accum_out=small[:, SUMC + par:SUMC + par + 1]), S["exp_ready"])
                            give_fill(act, ("s", li, m_, h, cc))
                        if li == 0:
                            mod_row(0, FIRST_MODS + HEADS * i + h)
                        if h:
                            probs_turned(h - 1)
                    probs_turned(HEADS - 1)
                    b = filled_bank(act, ("o", li, m_))
                    step(copy(a_o[:, m_, :], b), S["o_copied"])
                    give_fill(act, ("o", li, m_))
                stat_root(li, 2, sm(O_STAT, 16), P)
                turned(li, "ya", ATT)
                step(copy(small[:, 700:701], one), act_left)

            def hyena(li):
                enter(act, ph(li, 2))
                for dst, src in ((HYB["w1"][0:HY_EMB, :], hy_w1[li]), (HYB["w2"][0:HY_HID, :], hy_w2[li]),
                                 (HYB["feats"], feats_table),
                                 (small[0:64, HYC:HYC + 1], hy_b1[li].unsqueeze(1)),
                                 (small[0:64, HYC + 1:HYC + 2], hy_b2[li].unsqueeze(1)),
                                 (small[0:64, HYC + 2:HYC + 3], hy_freq[li, 0].unsqueeze(1)),
                                 (small[0:64, HYC + 3:HYC + 4], hy_freq[li, 1].unsqueeze(1))):
                    act.dma_start(dst, src).then_inc(hyf_loaded, 16)
                for dst, src in ((HYB["w3"][0:HY_HID].rearrange("p a b -> p (a b)"), hy_w3[li]),
                                 (HYB["decay"].rearrange("p a b c -> p (a b c)"), decay),
                                 (HYB["bias"], hy_bias[li].unsqueeze(0).to_broadcast([P, 2, BR_W]))):
                    act.dma_start(dst, src).then_inc(hyw_loaded, 16)
                for i in range(2):
                    act.wait_ge(S["hyf_arg"], 2 * li + i + 1)
                    step(f(HYB["s"][0:HY_HID], HYB["arg"][0:HY_HID], ACT.Sin), S["hyf_sin"])
                act.wait_ge(S["hyf_done"], li + 1)
                tl = tiles(li)

                def u_copy(blk):
                    b = filled_bank(act, ("hyu", li, blk))
                    dst = HYB["u"][:, tl[0]:NT, blk // 4, (blk % 4) * P:(blk % 4 + 1) * P]
                    step(copy(dst, hd(b)[:, tl[0]:NT, :]), S["hy_u"])
                    give_fill(act, ("hyu", li, blk))
                n0 = first_strip["hy", li]
                for s_ in range(6):
                    hi_ahead(act, n0 + 2 * s_)
                    hi_ahead(act, n0 + 2 * s_ + 1)
                    if s_:
                        u_copy(2 * s_ - 2)
                        u_copy(2 * s_ - 1)
                u_copy(10)
                u_copy(11)
                turned(li, "yh", HY)
                step(copy(small[:, 700:701], one), act_left)

            def fnet(li):
                tk = toks(li)
                enter(act, ph(li, 3))
                act.dma_start(fn_tab, fn_table).then_inc(fnw_loaded, 16)
                n0 = first_strip["fn", li]
                for g in range(HEADS):
                    if g % 2 == 0:
                        hi_ahead(act, n0 + g)
                        hi_ahead(act, n0 + g + 1)
                    b = unit_bank_of(act, "fn", li, g)
                    step(copy(fn_u_[:, g, tk], b[:, tk]), S["fn_u"])
                    give_unit(act, "fn", li, g)
                for s_ in streams(li):
                    for g in range(HEADS):
                        b = filled_bank(act, ("fv", li, s_, g))
                        step(copy(fn_v_[:, s_, g].rearrange("p t n -> p (t n)"), b), S["fn_v"])
                        give_fill(act, ("fv", li, s_, g))
                for s_ in streams(li):
                    for g in range(HEADS):
                        b = filled_bank(act, ("fy", li, s_, g))
                        step(copy(y[:, FN, g, s_ * L:(s_ + 1) * L], b[:, 0:L]), S["y_turned"])
                        give_fill(act, ("fy", li, s_, g))
                step(copy(small[:, 700:701], one), act_left)

            def merge(li):
                tk = toks(li)
                enter(act, ph(li, 4))
                s0, u0, m0 = strip_loop("merge", li)
                ends = [strip_end[s0 + i] - m0 for i in range(12)]
                with act.Fori(0, N_BRANCH) as n:
                    act.wait_ge(unit_done, m0 + n * 20)
                    copy(y_hl[:, 0], y[:, bass.ds(n, 1)].rearrange("p a h t -> p (a h) t"))\
                        .then_inc(S["yhi_ready"], 1)
                    for i in range(12):
                        jj, j = i // 6, i % 6
                        split_hi(act, s0 + i + RING, n, 12, m0 + ends[i] + n * 20)
                        if j in (1, 3):
                            for cb in range(2):
                                g = j - 1 + cb
                                if g == 0:
                                    act.wait_ge(S["acc_added"], 34 * li + 2 + n * 8 + 4 * jj)
                                f(m_sg[:, g, tk], unit_bank[g][:, tk], ACT.Sigmoid).then_inc(S["sg_ready"], 1)
                                act.wait_ge(S["sg_ready"], 32 * li + n * 8 + 4 * jj + g + 1)
                                act.sem_inc(unit_free[g], 1)

            def mlp(li):
                tk = toks(li)
                for hf in range(2):
                    s0, u0, m0 = strip_loop(("mlp1", hf), li)
                    r0 = 16 * (2 * li + hf)
                    with act.Fori(0, 4) as i:
                        for e in range(2):
                            for kh in range(2):
                                split_hi(act, s0 + 2 * e + kh + RING, i, 4, m0 + 3 * e + (1, 3)[kh] + i * 6)
                            for cb in range(2):
                                g = 2 * e + cb
                                act.wait_ge(mlp_ready[cb], r0 // 2 + e + 1 + i * 2)
                                f(tmp[:, cb, tk], unit_bank[g][:, tk], ACT.Relu).then_inc(S["relu_ready"], 1)
                                act.wait_ge(S["relu_ready"], r0 + g + 1 + i * 4)
                                act.sem_inc(unit_free[g], 1)
                    s0, u0, m0 = strip_loop(("mlp2", hf), li)
                    last = li == DEPTH - 1 and hf == 1
                    with act.Fori(0, 3 if last else 4) as i:
                        for kc in range(4):
                            split_hi(act, s0 + kc + RING, i, 4, m0 + 2 * kc + 2 + i * 8)
                    if last:
                        for kc in range(4):
                            hi_ahead(act, s0 + 12 + kc)
                step(copy(small[:, 700:701], one), act_left)

            def wo(li):
                for i in range(8):
                    hi_ahead(act, first_strip["wo", li] + i)

            start_()
            for li in range(DEPTH):
                norm(li, 0)
                dn(li)
                att(li)
                hyena(li)
                fnet(li)
                merge(li)
                wo(li)
                norm(li, 1)
                mlp(li)
            enter(act, ph(DEPTH, 0))
            for i in range(4):
                b = filled_bank(act, ("out", i))
                step(copy(outs[:, i // 2, (i % 2) * 512:(i % 2 + 1) * 512], b), S["out_ready"])

        @block.vector
        def _(dve):
            V = nc.vector

            def step(ins, s_=dve_step):
                link(dve, ins, s_)

            def tt(o_, a, b, op, s_=dve_step):
                step(V.tensor_tensor(o_, a, b, op), s_)

            def ts(o_, a, s1, s2, op0, op1=None, s_=dve_step):
                if op1 is None:
                    step(V.tensor_scalar(o_, a, s1, None, op0), s_)
                else:
                    step(V.tensor_scalar(o_, a, s1, s2, op0, op1), s_)

            def stt(o_, a, sc, b, op0, op1, s_=dve_step):
                step(V.scalar_tensor_tensor(o_, a, sc, b, op0, op1), s_)

            def cp(o_, a, s_=dve_step):
                step(V.tensor_copy(o_, a), s_)

            ADD, MUL, SUB, MAX = ALU.add, ALU.mult, ALU.subtract, ALU.max

            def start_():
                split_lo(dve, 0)
                split_lo(dve, 1)
                for li in range(DEPTH):
                    b = filled_bank(dve, ("cols", li))
                    n = 52 if li == 0 else 36
                    cp(cols[:, li, 0, 0:100], b[:, 0:100])
                    cp(cols[:, li, 1, 0:n], b[:, 128:128 + n], S["cols_ready"])
                    give_fill(dve, ("cols", li))
                    if li == 0:
                        dve.wait_ge(S["cT_ready"], 2)
                        tt(chl[:, 1], csil[:], chl[:, 0].bitcast(F32), SUB)
                        cp(small[:, 0:1], one, S["clo_ready"])
                        step(V.memset(tmp[:, 0, 0:1], 0.0), mlp_ready[0])
                        step(V.memset(tmp[:, 1, 0:1], 0.0), mlp_ready[1])
                for g in range(FIRST_MODS):
                    lo_ahead(dve, first_strip[("mod", g), 0])
                    lo_ahead(dve, first_strip[("mod", g), 0] + 1)
                    if g:
                        mod_cols(0, g - 1)
                mod_cols(0, FIRST_MODS - 1)
                amps(0, 0)

            def mod_cols(li, g):
                b = filled_bank(dve, ("mod", li, g))
                tt(mod[:, li, 2 * g:2 * g + 2, :], b[:, 0:4].rearrange("p (f s) -> p f s", s=2),
                   cols[:, li, 0, 2 * g:2 * g + 2].unsqueeze(2).to_broadcast([P, 2, 2]), ADD)
                give_fill(dve, ("mod", li, g))

            def amps(li, w):
                stt(amp[:, li, w], mod[:, li, 24 * w + 8:24 * w + 16, :], 1.0,
                    cols[:, li, 0, 48 + 8 * w:56 + 8 * w].unsqueeze(2).to_broadcast([P, KD, 2]), ADD, MUL)

            def norm(li, which):
                nn = 2 * li + which
                if which == 0:
                    dve.wait_ge(vecs_loaded, 7 * 16 * (li + 1))
                    cp(wab_hl[:, 0], wab[:])
                    tt(wab_hl[:, 1], wab[:], wab_hl[:, 0].bitcast(F32), SUB, S["wab_split"])
                dve.wait_ge(S["rstd_ready"], nn + 1)
                ss = range(2) if which == 0 else streams(li)

                def low(k):
                    dve.wait_ge(S["hhi_ready"], KD * nn + k + 1)
                    for s_ in ss:
                        sl = slice(s_ * L, (s_ + 1) * L)
                        ins = V.scalar_tensor_tensor(hhl[:, 1, k, sl], tmp[:, k % 2, sl],
                                                     mod[:, li, 24 * which + k, s_:s_ + 1],
                                                     hhl[:, 0, k, sl].bitcast(F32), ADD, SUB)
                    step(ins, S["h_ready"] if k == KD - 1 else dve_step)
                for k in range(KD):
                    for s_ in ss:
                        sl = slice(s_ * L, (s_ + 1) * L)
                        ins = V.scalar_tensor_tensor(tmp[:, k % 2, sl], xT[:, k, sl],
                                                     amp[:, li, which, k, s_:s_ + 1], rstd[:, sl], MUL, MUL)
                    ins.then_inc(S["hn_ready"], 1)
                    if k:
                        low(k - 1)
                low(KD - 1)

            def conv(key, li, blk, dst, base, tk):
                b = unit_bank_of(dve, key, li, blk)
                w = [cols[:, li, 0 if key == "hy" else 1, base + 12 * i + blk:base + 12 * i + blk + 1] for i in range(3)]
                p3 = b[:, tk].rearrange("p (s t) -> p s t", t=L)
                d3 = dst[:, tk].rearrange("p (s t) -> p s t", t=L)
                ts(d3, p3, w[1], None, MUL)
                stt(d3[:, :, 1:L], p3[:, :, 0:L - 1], w[0], d3[:, :, 1:L], MUL, ADD)
                stt(d3[:, :, 0:L - 1], p3[:, :, 1:L], w[2], d3[:, :, 0:L - 1], MUL, ADD, S["block_conv"])
                give_unit(dve, key, li, blk)

            def t8(v):
                return v.rearrange("p (t e) -> p t e", t=NT)

            def dn(li):
                dve.wait_ge(vecs_loaded, 7 * 16 * (li + 1))
                b = filled_bank(dve, ("dab", li))[:, 0:64].rearrange("p (t e) -> p t e", t=NT)
                tt(t8(sm(SC)), b[:, :, 0:8], dtb.unsqueeze(1).to_broadcast([P, NT, 8]), ADD)
                cp(t8(sm(SC + 96)), b[:, :, 8:16])
                give_fill(dve, ("dab", li))
                ts(sm(SC + 64), sm(SC), 0.0, None, MAX)
                stt(sm(SC + 32), sm(SC), -1.0, sm(SC), MUL, ALU.min, S["gate_cols"])
                for blk in range(12):
                    conv("dn", li, blk, qkvT[:, blk], 0, slice(0, T))
                    if blk == 1:
                        dve.wait_ge(S["decays_ready"], 2 * li + 1)
                        tt(sm(SC), sm(SC + 64), sm(SC + 32), ADD)
                        stt(t8(sm(G_)), t8(sm(SC)), -1.0, small[:, HYC:HYC + 8].unsqueeze(1)
                            .to_broadcast([P, NT, 8]), MUL, MUL)
                        ts(sm(SC + 96), sm(SC + 96), 1.0, None, ADD)
                        step(V.reciprocal(sm(BETA), sm(SC + 96)), S["g_ready"])
                b = filled_bank(dve, ("gcum", li))
                cp(sm(GC, 64), b[:, 0:64])
                give_fill(dve, ("gcum", li))
                tt(sm(GC + 64), sm(GC + 32), sm(GC), SUB, S["gate_cols"])
                for blk in range(8):
                    dve.wait_ge(S["block_rstd"], 8 * li + blk + 1)
                    v = qkvT[:, blk, :]
                    stt(v, v, P ** -0.5 if blk < 4 else 1.0, tmp[:, blk % 2, :], MUL, MUL, S["block_normed"])
                dve.wait_ge(S["decays_ready"], 2 * li + 2)
                tt(sm(BEG), sm(EGC), sm(BETA), MUL)
                for st in range(4):
                    q = 4 * li + st
                    sc = [(d, DS[d], MT[d][st], filled_bank) for d in range(2)]

                    def col4(a, m_, d):
                        return bc_heads(small[:, a + 8 * m_ + 4 * d:a + 8 * m_ + 4 * d + 4])
                    for d in range(2):
                        s_, m_ = DS[d], MT[d][st]
                        b = filled_bank(dve, ("gcb", q, d))
                        tt(hd(s_["dI"]), hd(b), over_heads(const(f"far{d}")), ADD, SD["far_ready"][d])
                        give_fill(dve, ("gcb", q, d))

                    def weave(i):
                        if li == 0 and i:
                            mod_cols(1, i - 1)
                    weave(6 * st)
                    for d in range(2):
                        s_, m_ = DS[d], MT[d][st]
                        dve.wait_ge(SD["dI_ready"][d], q + 1)
                        for h in range(HEADS):
                            hs = slice(h * P, (h + 1) * P)
                            col = BETA + 8 * m_ + 4 * d + h
                            b = filled_bank(dve, (f"kq{h // 2}", q, d)).rearrange("p (h e n) -> p h e n", h=2, e=2)
                            stt(s_["A"][:, hs], b[:, h % 2, 1, :], small[:, col:col + 1], s_["dI"][:, hs], MUL, MUL,
                                SD["A_ready"][d] if h == 3 else dve_step)
                    for d in range(2):
                        s_ = DS[d]
                        dve.wait_ge(SD["copied"][d], NC_ * q + 1)
                        for hp in range(2):
                            b = filled_bank(dve, (f"kq{hp}", q, d)).rearrange("p (h e n) -> p h e n", h=2, e=2)
                            v = hd(s_["ITt"])[:, 2 * hp:2 * hp + 2, :]
                            tt(v, v, b[:, :, 0, :], MUL, SD["IT_ready"][d] if hp else dve_step)
                            give_fill(dve, (f"kq{hp}", q, d))
                        tt(hd(s_["dI"]), hd(s_["A"]), over_heads(const(f"blk{d}")), MUL, SD["blk_ready"][d])
                    for d in range(2):
                        s_ = DS[d]
                        b = filled_bank(dve, ("B", q, d))
                        tt(hd(s_["Un"]), hd(b), over_heads(const(f"blk{1 - d}")), MUL, SD["blk_ready"][d])
                        give_fill(dve, ("B", q, d))
                        tt(hd(s_["U"]), over_heads(ident), hd(s_["Un"]), SUB, SD["blk_ready"][d])

                    weave(6 * st + 1)
                    for d in range(2):
                        s_ = DS[d]
                        for hp in range(2):
                            b = filled_bank(dve, (f"BU{hp}", q, d)).rearrange("p (h e n) -> p h e n", h=2, e=2)
                            two = slice(2 * hp, 2 * hp + 2)
                            cp(hd(s_["P4"])[:, two, :], b[:, :, 0, :])
                            tt(hd(s_["Un"])[:, two, :], hd(s_["U"])[:, two, :], b[:, :, 1, :], ADD,
                               SD["U_ready"][d] if hp else dve_step)
                            give_fill(dve, (f"BU{hp}", q, d))
                    weave(6 * st + 2)
                    for nm, cur, nxt, op in (("Ub", "Un", "U", ADD), ("Uc", "U", "Un", ADD),
                                             ("M0", "Un", "U", SUB), ("M1", "U", "Un", SUB), ("M2", "Un", "U", SUB)):
                        if nm in ("Uc", "M1", "M2"):
                            weave(6 * st + {"Uc": 3, "M1": 4, "M2": 5}[nm])
                        for d in range(2):
                            s_ = DS[d]
                            b = filled_bank(dve, (nm, q, d))
                            tt(s_[nxt], s_[cur], b, op, SD["U_ready"][d])
                            give_fill(dve, (nm, q, d))
                    for d in range(2):
                        s_, m_ = DS[d], MT[d][st]
                        b = filled_bank(dve, ("KS", q, d))
                        tt(hd(s_["P4"]), hd(b), col4(BEG, m_, d), MUL)
                        give_fill(dve, ("KS", q, d))
                        dve.wait_ge(SD["vb_ready"][d], q + 1)
                        tt(s_["P1"], s_["P1"], s_["P4"], SUB, SD["r_ready"][d])
                        if reads_out(li, st):
                            b = filled_bank(dve, ("qS", q, d))
                            tt(hd(s_["P2"]), hd(b), col4(EGC, m_, d), MUL)
                            give_fill(dve, ("qS", q, d))
                    for d in range(2):
                        if not reads_out(li, st):
                            continue
                        s_, m_ = DS[d], MT[d][st]
                        if st % 2:
                            tt(s_["P2"], s_["P2"], o_dn[:, m_, :], ADD)
                        b = filled_bank(dve, ("iv", q, d))
                        tt(o_dn[:, m_, :], s_["P2"], b, ADD, SD["o_added"][d])
                        give_fill(dve, ("iv", q, d))
                    if st < 3:
                        for d in range(2):
                            s_, m_ = DS[d], MT[d][st]
                            b = filled_bank(dve, ("kv", q, d))
                            tt(hd(s_["S"]), hd(s_["S"]), col4(ETOT, m_, d), MUL)
                            tt(s_["S"], s_["S"], b, ADD, SD["S_ready"][d])
                            give_fill(dve, ("kv", q, d))
                if li == 0:
                    mod_cols(1, MODGROUPS - 1)
                    amps(1, 0)
                    amps(1, 1)
                token_norm(li, 0, o_dn, dnnorm, DN, DS[1]["A"])
                cp(small[:, 701:702], one, dve_left)

            def token_norm(li, i, o_, gain, br, scratch):
                for m_ in tiles(li):
                    tt(scratch, o_[:, m_, :], o_[:, m_, :], MUL)
                    step(V.tensor_reduce(small[:, O_STAT + 4 * m_:O_STAT + 4 * m_ + 4], hd(scratch), AX, ADD),
                         S["stat_ready"] if m_ == NT - 1 else dve_step)
                dve.wait_ge(S["stat_root"], 3 * li + i + 1)
                if br == DN:
                    dve.wait_ge(S["token_copied"], (0 if li == 0 else 16) + (4 if li == 0 else 2))
                for m_ in tiles(li):
                    v = hd(o_[:, m_, :])
                    tt(v, v, bc_heads(small[:, O_STAT + 4 * m_:O_STAT + 4 * m_ + 4]), MUL)
                    if br == DN:
                        tt(o_[:, m_, :], o_[:, m_, :], dz_tok[:, m_, :], MUL)
                    tt(v, v, over_heads(gain), MUL, S["o_normed"])

            def att(li):
                lam_init = 0.8 - 0.6 * math.exp(-0.3 * li)
                enter(dve, ph(li, 1))
                l4 = lamv.rearrange("p (a b n) -> p a b n", a=2, b=2)
                sq = a_sq[:, 0, 0:128].rearrange("p (a n) -> p a n", a=2)
                tt(sq, l4[:, :, 0, :], l4[:, :, 1, :], MUL)
                step(V.tensor_reduce(sm(LAM, 2), sq, AX, ADD))
                ts(subln, subln, 1.0 - lam_init, None, MUL)
                dve.wait_ge(S["token_copied"], 12 if li == 0 else 16 + 8)
                for which in range(2):
                    tl = tiles(li) if which == 0 else range(NT)
                    for m_ in tl:
                        v = a_qk[:, which, m_, :]
                        tt(a_sq[:, 0, :], v, v, MUL)
                        c0 = QK_STAT + 8 * (4 * which + m_)
                        step(V.tensor_reduce(small[:, c0:c0 + 8], a_sq[:, 0, :].rearrange("p (g n) -> p g n", g=8),
                                             AX, ADD), S["stat_ready"] if (which, m_) == (1, NT - 1) else dve_step)
                dve.wait_ge(S["stat_root"], 3 * li + 2)
                tt(sm(LAM + 2, 1), sm(LAM + 1, 1), sm(LAM, 1), SUB)
                ts(sm(LAM + 3, 1), sm(LAM + 2, 1), -lam_init, None, ADD)
                scale_and_turn(dve, step, 1, range(NT), a_sq, S["k_ready"])
                for i, m_ in enumerate(tiles(li)):
                    nk = 2 if m_ < 2 else 4

                    def combine(h):
                        n = att_n(li, i, h)
                        par = n % 2
                        dve.wait_ge(S["exp_ready"], 2 * n + 2)
                        r = small[:, SUMC + 2 * par:SUMC + 2 * par + 2]
                        step(V.reciprocal(r, r))
                        tt(r[:, 1:2], r[:, 1:2], sm(LAM + 3, 1), MUL)
                        p = a_P[:, h % 2]
                        ks = slice(0, nk * P)
                        ts(p[:, 0, ks], p[:, 0, ks], r[:, 0:1], None, MUL)
                        stt(p[:, 0, ks], p[:, 1, ks], r[:, 1:2], p[:, 0, ks], MUL, ADD, S["a_ready"])
                    for h in range(HEADS):
                        n = att_n(li, i, h)
                        for cc in range(2):
                            par = 2 * (n % 2) + cc
                            b = filled_bank(dve, ("s", li, m_, h, cc))
                            step(V.tensor_reduce(small[:, MAXC + par:MAXC + par + 1], b[:, 0:nk * P], AX, MAX))
                            ts(small[:, MAXC + 8 + par:MAXC + 9 + par], small[:, MAXC + par:MAXC + par + 1], -0.125,
                               None, MUL, s_=S["max_ready"])
                        if h:
                            combine(h - 1)
                        if li == 0 and i + h:
                            mod_cols(0, FIRST_MODS + HEADS * i + h - 1)
                    combine(HEADS - 1)
                if li == 0:
                    mod_cols(0, MODGROUPS - 1)
                    amps(0, 1)
                dve.wait_ge(S["o_copied"], 4 if li == 0 else 6)
                token_norm(li, 2, a_o, subln, ATT, a_sq[:, 0, :])
                cp(small[:, 701:702], one, dve_left)

            def hyena(li):
                enter(dve, ph(li, 2))
                H_ = HYB
                for i in range(2):
                    b = filled_bank(dve, (f"f{i + 1}", li))
                    dve.wait_ge(hyf_loaded, HYF * (li + 1))
                    a = H_["arg"][0:HY_HID]
                    k = H_["turns"][0:HY_HID]
                    ts(a, b[0:HY_HID, 0:L], small[0:64, HYC + i:HYC + i + 1], small[0:64, HYC + 2 + i:HYC + 3 + i], ADD, MUL)
                    give_fill(dve, (f"f{i + 1}", li))
                    ts(k, a, 1 / (2 * math.pi), None, MUL)
                    ts(k, k, ROUND, None, ADD)
                    ts(k, k, ROUND, None, SUB)
                    for part in TWO_PI:
                        stt(a, k, -part, a, MUL, ADD)
                    ts(a, a, -3.1415925, 3.1415925, MAX, ALU.min, s_=S["hyf_arg"])
                dve.wait_ge(hyw_loaded, HYW * (li + 1))
                for n in range(2):
                    K = H_["K"][:, n]
                    for t_ in range(2):
                        for dr in range(2):
                            b = filled_bank(dve, ("f3", li, n, t_, dr))
                            tt(H_["z1"][:, 2 * t_ + dr, :], b, H_["decay"][:, t_, dr, :], MUL)
                            give_fill(dve, ("f3", li, n, t_, dr))
                    for t_ in range(2):
                        f0, f1 = H_["z1"][:, 2 * t_, :], H_["z1"][:, 2 * t_ + 1, :]
                        tt(H_["z0"][:, 2 * t_, :], f0, f1, ADD)
                        tt(H_["z0"][:, 2 * t_ + 1, :], f0, f1, SUB)
                    z1f = H_["z1"].rearrange("p a b -> p (a b)")
                    stt(z1f, z1f, -1.0, z1f, MUL, MAX, S["hyf_taps"])
                    b = filled_bank(dve, ("fs", li, n))
                    step(V.reciprocal(H_["inv"], b))
                    give_fill(dve, ("fs", li, n))
                    for fc in range(4):
                        b = filled_bank(dve, ("fk", li, n, fc))
                        tt(K[:, fc, :], b, H_["inv"], MUL)
                        give_fill(dve, ("fk", li, n, fc))
                    b = filled_bank(dve, ("fL", li, n))
                    cp(K[:, 4, :], K[:, 0, :])
                    tt(K[0:1, 4, :], b[0:1, :], H_["inv"][0:1, :], MUL)
                    give_fill(dve, ("fL", li, n))
                    step(V.memset(K[0:1, 2, :], 0.0), S["hyf_done"] if n else dve_step)
                for blk in range(12):
                    if blk >= 2:
                        dve.wait_ge(filled, fill_at["hyu", li, blk - 2] + 1)
                    conv("hy", li, blk, H_["cb"][:, blk % 2], 64, toks(li))
                dve.wait_ge(S["hy_u"], 12 * (li + 1))
                for n in range(2):
                    K = H_["K"][:, n]
                    for s_ in streams(li):
                        zz = hyz(li, n, s_)
                        z0, z1 = H_["z0"], H_["z1"]
                        for re, kr, ki, kr2 in ((0, 0, 2, 4), (1, 1, 3, 1)):
                            br, bi = (filled_bank(dve, ("zf", zz, re)), filled_bank(dve, ("zf", zz, re + 2)))
                            tt(z0[:, re, :], br, K[:, kr, :], MUL)
                            tt(z0[:, re + 2, :], br, K[:, ki, :], MUL)
                            give_fill(dve, ("zf", zz, re))
                            tt(z1[:, re, :], bi, K[:, ki, :], MUL)
                            tt(z1[:, re + 2, :], bi, K[:, kr2, :], MUL)
                            give_fill(dve, ("zf", zz, re + 2))
                            tt(z0[:, re, :], z0[:, re, :], z1[:, re, :], SUB)
                            tt(z0[:, re + 2, :], z0[:, re + 2, :], z1[:, re + 2, :], ADD, S["zf_ready"])
                        for t_ in range(2):
                            u = H_["u"][:, 2 * s_ + t_]
                            tt(H_["zt"], u[:, 2, :], H_["bias"][:, n, :], MUL)
                            b = filled_bank(dve, ("zt", zz, t_))
                            tt(H_["zt"], H_["zt"], b, ADD)
                            give_fill(dve, ("zt", zz, t_))
                            tt(u[:, 2, :], H_["zt"], u[:, n, :], MUL, S["z_ready"] if t_ else dve_step)
                cp(small[:, 701:702], one, dve_left)

            def merge(li):
                tk = toks(li)
                s0, u0, m0 = strip_loop("merge", li)
                cp(small[:, 701:702], one, dve_left)
                enter(dve, ph(li, 4))
                take_over(dve, "merge", li)
                with dve.Fori(0, N_BRANCH) as n:
                    dve.wait_ge(S["yhi_ready"], N_BRANCH * li + 1 + n)
                    V.tensor_tensor(y_hl[:, 1], y[:, bass.ds(n, 1)].rearrange("p a h t -> p (a h) t"),
                                    y_hl[:, 0].bitcast(F32), SUB).then_inc(S["ysplit"], 1)
                    for jj in range(2):
                        for j in range(4):
                            split_lo(dve, s0 + 6 * jj + j + RING, n, 12)
                        for g in range(4):
                            i = 4 * jj + g
                            if g % 2 == 0:
                                split_lo(dve, s0 + 6 * jj + 4 + g // 2 + RING, n, 12)
                            dve.wait_ge(unit_done, m0 + n * 20 + 10 * jj + 6 + g + 1)
                            dve.wait_ge(S["sg_ready"], 32 * li + n * 8 + 4 * jj + g + 1)
                            dve.wait_ge(S["acc_added"], 34 * li + 1 + n * 8 + i)
                            V.tensor_tensor(tmp[:, g % 2, tk], unit_bank[g][:, tk], m_sg[:, g, tk], MUL)\
                             .then_inc(S["mul_done"], 1)
                            dve.wait_ge(S["mul_done"], 32 * li + n * 8 + i + 1)
                            dve.sem_inc(unit_free[g], 1)
                dve.wait_ge(S["acc_added"], 34 * (li + 1))
                for k in range(KD):
                    cp(acc_hl[:, 0, k, tk], m_acc[:, k, tk])
                    tt(acc_hl[:, 1, k, tk], m_acc[:, k, tk], acc_hl[:, 0, k, tk].bitcast(F32), SUB,
                       S["acc_split"] if k == KD - 1 else dve_step)

            def residual(key, li, gate):
                n0, per = first_strip[key, li], (2 if key == "wo" else 4)
                for blk in range(KD):
                    if blk % 2 == 0:
                        for i in range(per):
                            lo_ahead(dve, n0 + per * (blk // 2) + i)
                    if key == "wo":
                        b = unit_bank_of(dve, key, li, blk)
                    else:
                        dve.wait_ge(unit_done, first_mark[key, li] + 8 * (blk // 2) + 7 + blk % 2)
                        b = unit_bank[blk % UNITS]
                    for s_ in streams(li):
                        sl = slice(s_ * L, (s_ + 1) * L)
                        ins = V.scalar_tensor_tensor(xT[:, blk, sl], b[:, sl], mod[:, li, gate + blk, s_:s_ + 1],
                                                     xT[:, blk, sl], MUL, ADD)
                    step(ins, S["x_added"])
                    dve.sem_inc(unit_free[(first_unit[key, li] + blk) % UNITS], 1)

            def mlp(li):
                tk = toks(li)
                for hf in range(2):
                    s0, u0, m0 = strip_loop(("mlp1", hf), li)
                    r0 = 16 * (2 * li + hf)
                    if hf:
                        dve.wait_ge(unit_done, strip_end[first_strip[("mlp2", 0), li] + 15])
                    with dve.Fori(0, 4) as i:
                        for e in range(2):
                            for kh in range(2):
                                split_lo(dve, s0 + 2 * e + kh + RING, i, 4)
                            square(dve, 0, li, hf, e, i)
                    residual(("mlp2", hf), li, 40)
                cp(small[:, 701:702], one, dve_left)

            start_()
            for li in range(DEPTH):
                norm(li, 0)
                dn(li)
                att(li)
                hyena(li)
                merge(li)
                residual("wo", li, 16)
                norm(li, 1)
                mlp(li)

        @block.gpsimd
        def _(pool):
            G = nc.gpsimd

            def step(ins, s_=pool_step):
                link(pool, ins, s_)

            def ahead(key, li):
                n0 = first_strip[key, li]
                count = {"dn": 12, "dz": 4, "aq": 4, "ak": 4, "av": 4, "hy": 12, "fn": 4, "wo": 8}[key]
                for n in range(n0, n0 + count):
                    lo_ahead(pool, n)

            def dn(li):
                take_over(pool, "dn", li)
                ahead("dn", li)
                pool.wait_ge(S["g_ready"], li + 1)
                for d in range(2):
                    step(G.memset(DS[d]["S"], 0.0), S["seg_ready"])
                def weave(i):
                    if li == 0:
                        for e in range(2):
                            lo_ahead(pool, first_strip[("mod", i), 1] + e)
                for st in range(4):
                    q = 4 * li + st

                    def col4(a, m_, d):
                        return bc_heads(small[:, a + 8 * m_ + 4 * d:a + 8 * m_ + 4 * d + 4])
                    for d in range(2):
                        m_ = MT[d][st]
                        if st:
                            pool.wait_ge(SD["S_ready"][d], q - li)
                        step(G.tensor_tensor(hd(DS[d]["P5"]), over_heads(const(f"tri{d}")), col4(G_, m_, d), ALU.mult),
                             SD["trig_ready"][d])
                    weave(6 * st)
                    weave(6 * st + 1)
                    if st == 0:
                        pool.wait_ge(S["decays_ready"], 2 * (li + 1))
                        pool.wait_ge(S["block_tok"], 8 * (li + 1))
                    for lv, cp_ in ((0, 3), (1, 7), (2, 9)):
                        for d in range(2):
                            m_, s_ = MT[d][st], DS[d]
                            pool.wait_ge(SD["copied"][d], NC_ * q + cp_)
                            pool.wait_ge(SD["A_ready"][d], q + 1)
                            step(G.tensor_tensor(hd(s_["dI"]), hd(s_["A"]), over_heads(const(f"off{32 << lv}")),
                                                 ALU.mult), SD["aoff_ready"][d])
                            if lv == 0:
                                step(G.tensor_tensor(hd(s_["IT"]), hd(k_tok[:, m_, :]), col4(EDL, m_, d), ALU.mult),
                                     SD["kdec_ready"][d])
                                pool.wait_ge(SD["U_ready"][d], 6 * q + 1)
                                step(G.tensor_tensor(hd(s_["P1"]), hd(v_tok[:, m_, :]), col4(BETA, m_, d), ALU.mult),
                                     SD["vb_ready"][d])
                        if lv == 0:
                            weave(6 * st + 2)
                            weave(6 * st + 3)
                        else:
                            weave(6 * st + 3 + lv)

            def merge(li):
                tk = toks(li)
                enter(pool, ph(li, 4))
                for i in range(2):
                    step(G.memset(m_acc[:, 4 * i:4 * i + 4, :], 0.0), S["acc_added"])
                with pool.Fori(0, N_BRANCH) as n:
                    for i in range(KD):
                        pool.wait_ge(S["mul_done"], 32 * li + n * 8 + i + 1)
                        G.tensor_tensor(m_acc[:, i, tk], m_acc[:, i, tk], tmp[:, i % 2, tk], ALU.add)\
                         .then_inc(S["acc_added"], 1)
                pool.wait_ge(S["acc_added"], 34 * (li + 1))

            def mlp(li):
                for hf in range(2):
                    if hf:
                        pool.wait_ge(unit_done, strip_end[first_strip[("mlp2", 0), li] + 15])
                    with pool.Fori(0, 4) as i:
                        for e in range(2):
                            square(pool, 1, li, hf, e, i)

            for li in range(DEPTH):
                enter(pool, ph(li, 0))
                dn(li)
                step(G.memset(small[:, 702:703], 0.0), pool_left)
                for key in ("dz", "aq", "ak", "av"):
                    ahead(key, li)
                pool.wait_ge(S["stat_root"], 3 * li + 2)
                scale_and_turn(pool, step, 0, tiles(li), a_P[:, 0], S["q_ready"])
                for i in range(PHASES - 2):
                    step(G.memset(small[:, 702:703], 0.0), pool_left)
                if li == 0:
                    for g in range(FIRST_MODS, MODGROUPS):
                        for e in range(2):
                            lo_ahead(pool, first_strip[("mod", g), 0] + e)
                for key in ("hy", "fn"):
                    ahead(key, li)
                merge(li)
                mlp(li)
                step(G.memset(small[:, 702:703], 0.0), pool_left)
    return nc


_INS = ["x", "c", "ctx", "c_ctx", "w_ada", "b_ada", "norm1", "norm2", "w_in", "attn_qk_gain", "attn_lambda",
        "attn_subln", "hy_conv", "hy_w1", "hy_b1", "hy_freq", "hy_w2", "hy_b2", "hy_w3", "hy_bias", "dn_conv",
        "dn_a_log", "dn_dt_bias", "dn_norm", "w_gate", "w_branch", "w_o", "w_mlp1", "w_mlp2"]
_TABLES = ["table", "hy_table", "fn_table", "feats_table", "decay"]
_OUTS = [((1, L, D), "float32")]


def kernel(**inputs):
    import numpy as _np
    import concourse.bacc as _bacc
    from concourse import mybir as _mybir
    from concourse.bass_utils import run_bass_kernel_spmd as _run

    nc = _bacc.Bacc("TRN2", target_bir_lowering=False, num_devices=1)
    tables = dict(zip(_TABLES, constant_table()))
    arrays, args = {}, []
    for name in _INS + _TABLES:
        a = _np.ascontiguousarray(tables[name] if name in tables else inputs[name])
        arrays[f"in_{name}_dram"] = a
        args.append(nc.dram_tensor(f"in_{name}_dram", a.shape, _mybir.dt.from_np(a.dtype), kind="ExternalInput").ap())
    for i, (shape, dtype) in enumerate(_OUTS):
        dt = _mybir.dt.from_np(_np.dtype(dtype))
        args.append(nc.dram_tensor(f"out_{i}_dram", shape, dt, kind="ExternalOutput").ap())
    build(nc, *args)
    r = _run(nc, [arrays], core_ids=[0])
    got = tuple(r.results[0][f"out_{i}_dram"] for i in range(len(_OUTS)))
    return got[0]
```
